# Optimizing a Trainium2 kernel written in Bass

```python
import jax, jax.numpy as jnp
from jax import lax
import numpy as np

D_MODEL = 1024
BATCH = 1
SEQ = 256
DEPTH = 2

N_MEM = 256
ATT_GROUPS = ((128, 1), (512, 4), (2048, 16))
N_ATT_GROUPS = len(ATT_GROUPS)
ATT_HEADS = 4
ATT_HEAD_DIM = 128
ATT_WIDTH = ATT_HEADS * ATT_HEAD_DIM
Q_BLOCK = 128
HGRN_EXPAND = 128
HGRN_WIDTH = D_MODEL
HGRN_HEADS = HGRN_WIDTH // HGRN_EXPAND
HGRN_CHUNK = 64
D_FF = 2816
X_HEADS = 4
X_HEAD_DIM = D_MODEL // X_HEADS
ROPE_THETA = 10000.0
EPS = 1e-6
IN_SIZES = (N_ATT_GROUPS * ATT_WIDTH,) * 3 + (HGRN_WIDTH,) * 4 + (D_MODEL,) * 2
N_IN = sum(IN_SIZES)


def rms_norm(x, g):
    xf = x.astype(jnp.float32)
    y = xf * lax.rsqrt(jnp.mean(xf * xf, axis=-1, keepdims=True) + EPS)
    return (y * g.astype(jnp.float32)).astype(x.dtype)

def swiglu(h, w_gu, w_down):
    gate, up = jnp.split(h @ w_gu, 2, axis=-1)
    return (jax.nn.silu(gate) * up) @ w_down

def rope_tables(positions, dim, dtype):
    inv_freq = ROPE_THETA ** (-jnp.arange(0, dim, 2, dtype=jnp.float32) / dim)
    ang = positions.astype(jnp.float32)[..., None] * inv_freq
    cos = jnp.cos(ang)[:, :, None, None, :].astype(dtype)
    sin = jnp.sin(ang)[:, :, None, None, :].astype(dtype)
    return cos, sin

def apply_rope(x, cos, sin):
    x1, x2 = jnp.split(x, 2, axis=-1)
    return jnp.concatenate([x1 * cos - x2 * sin, x2 * cos + x1 * sin], axis=-1)

def dilated_attention(q, k, v):
    B, T, G, H, dh = q.shape
    n_blk = T // Q_BLOCK
    scale = dh ** -0.5
    k_groups = [k[:, :, gi] for gi in range(G)]
    v_groups = [v[:, :, gi] for gi in range(G)]

    def block(b):
        t0 = b * Q_BLOCK
        tq = t0 + jnp.arange(Q_BLOCK)
        q_blk = lax.dynamic_slice_in_dim(q, t0, Q_BLOCK, axis=1)
        outs, lses = [], []
        for gi, (window, dil) in enumerate(ATT_GROUPS):
            j = jnp.arange(window // dil + 1)
            idx = tq[:, None] - dil * j[None, :]
            valid = idx >= 0
            idx = jnp.maximum(idx, 0)
            k_sel = k_groups[gi][:, idx]
            v_sel = v_groups[gi][:, idx]
            s = jnp.einsum('bqhd,bqjhd->bqhj', q_blk[:, :, gi], k_sel,
                           preferred_element_type=jnp.float32) * scale
            s = jnp.where(valid[None, :, None, :], s, -jnp.inf)
            m = jnp.max(s, axis=-1, keepdims=True)
            p = jnp.exp(s - m)
            den = jnp.sum(p, axis=-1)
            o = jnp.einsum('bqhj,bqjhd->bqhd', p, v_sel.astype(jnp.float32)) / den[..., None]
            outs.append(o)
            lses.append(m[..., 0] + jnp.log(den))
        w = jax.nn.softmax(jnp.stack(lses, axis=-1), axis=-1)
        o = jnp.einsum('bqhgd,bqhg->bqhd', jnp.stack(outs, axis=-2), w)
        return o.astype(q.dtype)

    o = lax.map(block, jnp.arange(n_blk))
    return o.transpose(1, 0, 2, 3, 4).reshape(B, T, H * dh)

def hgrn2_recurrence(q, f_logit, i, lb):
    B, T, H, N = q.shape
    C = HGRN_CHUNK
    NC = T // C
    lb = lb.reshape(H, N).astype(jnp.float32)
    f = lb + (1.0 - lb) * jax.nn.sigmoid(f_logit.astype(jnp.float32))
    g = jnp.log(f)
    k = 1.0 - f
    qs = q.astype(jnp.float32) * (N ** -0.5)

    def to_chunks(a):
        return a.reshape(B, NC, C, H, a.shape[-1]).transpose(1, 0, 3, 2, 4)

    causal = jnp.tril(jnp.ones((C, C), dtype=bool))

    def step(S, inp):
        qc, kc, vc, gc = inp
        b = jnp.cumsum(gc, axis=2)
        diff = b[:, :, :, None, :] - b[:, :, None, :, :]
        decay = jnp.exp(jnp.where(causal[:, :, None], diff, -jnp.inf))
        A = jnp.einsum('bhtn,bhsn,bhtsn->bhts', qc, kc, decay)
        o = (jnp.einsum('bhts,bhsv->bhtv', A, vc)
             + jnp.einsum('bhtn,bhnv->bhtv', qc * jnp.exp(b), S))
        b_last = b[:, :, -1:, :]
        S = (jnp.exp(b_last[:, :, 0, :])[..., None] * S
             + jnp.einsum('bhsn,bhsv->bhnv', kc * jnp.exp(b_last - b), vc))
        return S, o

    S0 = jnp.zeros((B, H, N, i.shape[-1]), jnp.float32)
    _, o = lax.scan(step, S0, (to_chunks(qs), to_chunks(k),
                               to_chunks(i.astype(jnp.float32)), to_chunks(g)))
    return o.transpose(1, 0, 3, 2, 4).reshape(B, T, H, -1)

def cross_attention(h, mem_n, wq, wkv, wo):
    B, T, _ = h.shape
    M = mem_n.shape[1]
    q = (h @ wq).reshape(B, T, X_HEADS, X_HEAD_DIM)
    k, v = jnp.split(mem_n @ wkv, 2, axis=-1)
    k = k.reshape(B, M, X_HEADS, X_HEAD_DIM)
    v = v.reshape(B, M, X_HEADS, X_HEAD_DIM)
    s = jnp.einsum('bthd,bmhd->bhtm', q, k, preferred_element_type=jnp.float32) * (X_HEAD_DIM ** -0.5)
    p = jax.nn.softmax(s, axis=-1)
    o = jnp.einsum('bhtm,bmhd->bthd', p, v.astype(jnp.float32)).astype(h.dtype)
    return o.reshape(B, T, X_HEADS * X_HEAD_DIM) @ wo

def first_inputs(seed: int = 0) -> dict:
    key = jax.random.key(seed)
    ks = iter(jax.random.split(key, 32))
    f32 = jnp.float32

    def w(shape, fan_in):
        return jax.random.normal(next(ks), shape, f32) * (fan_in ** -0.5)

    def gain(shape):
        return 1.0 + 0.02 * jax.random.normal(next(ks), shape, f32)

    L = DEPTH
    return {
        "x": jax.random.normal(next(ks), (BATCH, SEQ, D_MODEL), f32),
        "mem": jax.random.normal(next(ks), (BATCH, N_MEM, D_MODEL), f32),
        "positions": jnp.broadcast_to(jnp.arange(SEQ, dtype=jnp.int32), (BATCH, SEQ)),
        "ffn1_norm": gain((L, D_MODEL)),
        "ffn1_w_gu": w((L, D_MODEL, 2 * D_FF), D_MODEL),
        "ffn1_w_down": w((L, D_FF, D_MODEL), D_FF),
        "mix_norm": gain((L, D_MODEL)),
        "w_in": w((L, D_MODEL, N_IN), D_MODEL),
        "hgrn_lower_bounds": 0.1 * jax.random.normal(next(ks), (L, HGRN_WIDTH), f32),
        "hgrn_head_norm": gain((L, HGRN_WIDTH)),
        "w_att_branch": w((L, ATT_WIDTH, D_MODEL), ATT_WIDTH),
        "w_hgrn_branch": w((L, HGRN_WIDTH, D_MODEL), HGRN_WIDTH),
        "w_mix_out": w((L, D_MODEL, D_MODEL), D_MODEL),
        "xattn_norm": gain((L, D_MODEL)),
        "mem_norm": gain((L, D_MODEL)),
        "xattn_wq": w((L, D_MODEL, X_HEADS * X_HEAD_DIM), D_MODEL),
        "xattn_wkv": w((L, D_MODEL, 2 * X_HEADS * X_HEAD_DIM), D_MODEL),
        "xattn_wo": w((L, X_HEADS * X_HEAD_DIM, D_MODEL), X_HEADS * X_HEAD_DIM),
        "ffn2_norm": gain((L, D_MODEL)),
        "ffn2_w_gu": w((L, D_MODEL, 2 * D_FF), D_MODEL),
        "ffn2_w_down": w((L, D_FF, D_MODEL), D_FF),
        "final_norm": gain((D_MODEL,)),
    }

def first_block(x, mem, positions, ffn1_norm, ffn1_w_gu, ffn1_w_down, mix_norm, w_in,
              hgrn_lower_bounds, hgrn_head_norm, w_att_branch, w_hgrn_branch, w_mix_out,
              xattn_norm, mem_norm, xattn_wq, xattn_wkv, xattn_wo,
              ffn2_norm, ffn2_w_gu, ffn2_w_down, final_norm):
    B, T, _ = x.shape
    cos, sin = rope_tables(positions, ATT_HEAD_DIM, x.dtype)
    lb_p = jax.nn.softmax(hgrn_lower_bounds.astype(jnp.float32), axis=0)
    lb_all = jnp.cumsum(lb_p, axis=0) - lb_p[0]
    split_at = [sum(IN_SIZES[:n]) for n in range(1, len(IN_SIZES))]

    for l in range(DEPTH):
        x = x + 0.5 * swiglu(rms_norm(x, ffn1_norm[l]), ffn1_w_gu[l], ffn1_w_down[l])

        h = rms_norm(x, mix_norm[l])
        z = h @ w_in[l]
        q_a, k_a, v_a, q_b, f_b, i_b, og_b, gate_a, gate_b = jnp.split(z, split_at, axis=-1)
        att_shape = (B, T, N_ATT_GROUPS, ATT_HEADS, ATT_HEAD_DIM)
        q_a = apply_rope(q_a.reshape(att_shape), cos, sin)
        k_a = apply_rope(k_a.reshape(att_shape), cos, sin)
        v_a = v_a.reshape(att_shape)
        y_a = dilated_attention(q_a, k_a, v_a) @ w_att_branch[l]

        hg_shape = (B, T, HGRN_HEADS, HGRN_EXPAND)
        o_b = hgrn2_recurrence(q_b.reshape(hg_shape), f_b.reshape(hg_shape),
                               i_b.reshape(hg_shape), lb_all[l])
        o_b = rms_norm(o_b, hgrn_head_norm[l].reshape(HGRN_HEADS, HGRN_EXPAND))
        o_b = o_b.reshape(B, T, HGRN_WIDTH).astype(x.dtype) * jax.nn.silu(og_b)
        y_b = o_b @ w_hgrn_branch[l]

        merged = jax.nn.sigmoid(gate_a) * y_a + jax.nn.sigmoid(gate_b) * y_b
        x = x + merged @ w_mix_out[l]

        x = x + cross_attention(rms_norm(x, xattn_norm[l]), rms_norm(mem, mem_norm[l]),
                                xattn_wq[l], xattn_wkv[l], xattn_wo[l])

        x = x + 0.5 * swiglu(rms_norm(x, ffn2_norm[l]), ffn2_w_gu[l], ffn2_w_down[l])

    return rms_norm(x, final_norm)


HEAD_DIM = 64
D_MIX = D_MODEL
N_HEADS_A = 4
N_HEADS_B = 4
N_HEADS_C = D_MIX // HEAD_DIM - N_HEADS_A - N_HEADS_B
ROPE_DIM = HEAD_DIM // 4
ROPE_THETA_2 = 500000.0
MOBA_BLOCK = 256
MOBA_TOPK = 3
DSA_TOPK = 256
IDX_HEADS = 8
IDX_DIM = 64
N_MOD = 9
RMS_EPS = 1e-6
NEG = -1e30


SPLIT_SIZES = (N_HEADS_A * HEAD_DIM, N_HEADS_A * HEAD_DIM, N_HEADS_A * HEAD_DIM,
               N_HEADS_B * HEAD_DIM, N_HEADS_B * HEAD_DIM, N_HEADS_B * HEAD_DIM,
               IDX_HEADS * IDX_DIM, IDX_DIM, IDX_HEADS,
               N_HEADS_C * HEAD_DIM, N_HEADS_C * HEAD_DIM, N_HEADS_C * HEAD_DIM)
D_IN = sum(SPLIT_SIZES)

def _rms(x):
    xf = x.astype(jnp.float32)
    return (xf * lax.rsqrt(jnp.mean(xf * xf, axis=-1, keepdims=True) + RMS_EPS))

def rmsnorm(x, g):
    return (_rms(x) * g.astype(jnp.float32)).astype(x.dtype)

def modulate(h, shift, scale):
    return h * (1 + scale) + shift

def swiglu_2(h, w1, w3, w2):
    return (jax.nn.silu(h @ w1) * (h @ w3)) @ w2

def rope_tables_2(seq):
    pos = jnp.arange(seq, dtype=jnp.float32)
    inv = ROPE_THETA_2 ** (-jnp.arange(0, ROPE_DIM, 2, dtype=jnp.float32) / ROPE_DIM)
    ang = pos[:, None] * inv[None, :]
    return jnp.cos(ang), jnp.sin(ang)

def apply_partial_rope(x, cos, sin):
    half = ROPE_DIM // 2
    xf = x.astype(jnp.float32)
    x1, x2 = xf[..., :half], xf[..., half:ROPE_DIM]
    c, s = cos[None, :, None, :], sin[None, :, None, :]
    out = jnp.concatenate([x1 * c - x2 * s, x2 * c + x1 * s, xf[..., ROPE_DIM:]], axis=-1)
    return out.astype(x.dtype)

def _chunk(a, n):
    return jnp.moveaxis(a.reshape(a.shape[0], n, Q_BLOCK, *a.shape[2:]), 1, 0)

def _unchunk(a):
    a = jnp.moveaxis(a, 0, 1)
    return a.reshape(a.shape[0], a.shape[1] * a.shape[2], *a.shape[3:])

def moba_attention(q, k, v):
    B, S, H, d = q.shape
    nb = -(-S // MOBA_BLOCK)
    pad = nb * MOBA_BLOCK - S
    kp = jnp.pad(k, ((0, 0), (0, pad), (0, 0), (0, 0)))
    vp = jnp.pad(v, ((0, 0), (0, pad), (0, 0), (0, 0)))
    kb = kp.reshape(B, nb, MOBA_BLOCK, H, d)
    vb = vp.reshape(B, nb, MOBA_BLOCK, H, d)
    kmean = jnp.mean(kb.astype(jnp.float32), axis=2)
    kbt = jnp.transpose(kb, (0, 3, 1, 2, 4))
    vbt = jnp.transpose(vb, (0, 3, 1, 2, 4))
    n_sel = min(MOBA_TOPK, max(nb - 1, 1))
    scale = HEAD_DIM ** -0.5
    nq = S // Q_BLOCK
    gather_blocks = jax.vmap(jax.vmap(lambda blk, ii: blk[ii]))

    def one_block(args):
        qi, ci = args
        t = ci * Q_BLOCK + jnp.arange(Q_BLOCK)
        cur = (ci * Q_BLOCK) // MOBA_BLOCK
        gate = jnp.einsum('bqhd,bnhd->bqhn', qi.astype(jnp.float32), kmean)
        gate = jnp.where(jnp.arange(nb) < cur, gate, NEG)
        _, idx = lax.top_k(gate, n_sel)
        valid = jnp.transpose(idx < cur, (0, 2, 1, 3))
        idx_t = jnp.transpose(idx, (0, 2, 1, 3))
        ksel = gather_blocks(kbt, idx_t)
        vsel = gather_blocks(vbt, idx_t)
        qh = jnp.transpose(qi, (0, 2, 1, 3))
        s_past = jnp.einsum('bhqd,bhqnkd->bhqnk', qh, ksel).astype(jnp.float32) * scale
        s_past = jnp.where(valid[..., None], s_past, NEG)
        kown = lax.dynamic_slice_in_dim(kp, cur * MOBA_BLOCK, MOBA_BLOCK, axis=1)
        vown = lax.dynamic_slice_in_dim(vp, cur * MOBA_BLOCK, MOBA_BLOCK, axis=1)
        s_own = jnp.einsum('bhqd,bkhd->bhqk', qh, kown).astype(jnp.float32) * scale
        kpos = cur * MOBA_BLOCK + jnp.arange(MOBA_BLOCK)
        s_own = jnp.where(kpos[None, :] <= t[:, None], s_own, NEG)
        n_past = n_sel * MOBA_BLOCK
        s = jnp.concatenate([s_past.reshape(B, H, Q_BLOCK, n_past), s_own], axis=-1)
        p = jax.nn.softmax(s, axis=-1).astype(v.dtype)
        p_past = p[..., :n_past].reshape(B, H, Q_BLOCK, n_sel, MOBA_BLOCK)
        p_own = p[..., n_past:]
        return (jnp.einsum('bhqnk,bhqnkd->bqhd', p_past, vsel)
                + jnp.einsum('bhqk,bkhd->bqhd', p_own, vown))

    out = lax.map(one_block, (_chunk(q, nq), jnp.arange(nq)))
    return _unchunk(out)

def dsa_attention(q, k, v, q_idx, k_idx, w_idx):
    B, S, H, d = q.shape
    topk = min(DSA_TOPK, S // 4)
    scale = HEAD_DIM ** -0.5
    nq = S // Q_BLOCK
    kf = k.reshape(B, S, H * d)
    vf = v.reshape(B, S, H * d)
    kix = k_idx.astype(jnp.float32)
    gather_rows = jax.vmap(lambda rows, ii: rows[ii])

    def one_block(args):
        qb, qib, wib, ci = args
        t = ci * Q_BLOCK + jnp.arange(Q_BLOCK)
        logits = jnp.einsum('bqjd,bsd->bqjs', qib.astype(jnp.float32), kix)
        score = jnp.einsum('bqj,bqjs->bqs', wib.astype(jnp.float32), jax.nn.relu(logits))
        score = jnp.where(jnp.arange(S)[None, :] <= t[:, None], score, NEG)
        _, sel = lax.top_k(score, topk)
        valid = sel <= t[None, :, None]
        ksel = gather_rows(kf, sel).reshape(B, Q_BLOCK, topk, H, d)
        vsel = gather_rows(vf, sel).reshape(B, Q_BLOCK, topk, H, d)
        s = jnp.einsum('bqhd,bqkhd->bhqk', qb, ksel).astype(jnp.float32) * scale
        s = jnp.where(valid[:, None, :, :], s, NEG)
        p = jax.nn.softmax(s, axis=-1).astype(v.dtype)
        return jnp.einsum('bhqk,bqkhd->bqhd', p, vsel)

    out = lax.map(one_block, (_chunk(q, nq), _chunk(q_idx, nq), _chunk(w_idx, nq), jnp.arange(nq)))
    return _unchunk(out)

def stick_breaking_attention(q, k, v):
    B, S, H, d = q.shape
    scale = HEAD_DIM ** -0.5
    nq = S // Q_BLOCK
    kpos = jnp.arange(S)

    def one_block(args):
        qb, ci = args
        t = ci * Q_BLOCK + jnp.arange(Q_BLOCK)
        z = jnp.einsum('bqhd,bshd->bhqs', qb, k).astype(jnp.float32) * scale
        strict = kpos[None, :] < t[:, None]
        log_beta = jax.nn.log_sigmoid(z)
        log_1m = jnp.where(strict, jax.nn.log_sigmoid(-z), 0.0)
        after = lax.cumsum(log_1m, axis=3, reverse=True) - log_1m
        a = jnp.where(strict, jnp.exp(log_beta + after), 0.0).astype(v.dtype)
        return jnp.einsum('bhqs,bshd->bqhd', a, v)

    out = lax.map(one_block, (_chunk(q, nq), jnp.arange(nq)))
    return _unchunk(out)

def second_inputs(seed: int = 0) -> dict:
    key = jax.random.key(seed)
    ks = jax.random.split(key, 12)
    f32 = jnp.float32
    x = jax.random.normal(ks[0], (BATCH, SEQ, D_MODEL), f32)
    c = jax.random.normal(ks[1], (BATCH, D_MODEL), f32)
    w_ada = jax.random.normal(ks[2], (DEPTH, D_MODEL, N_MOD * D_MODEL), f32) * D_MODEL ** -0.5
    b_ada = 0.01 * jax.random.normal(ks[3], (DEPTH, N_MOD * D_MODEL), f32)
    norm_g = 1.0 + 0.02 * jax.random.normal(ks[4], (DEPTH, 3, D_MODEL), f32)
    w_in = jax.random.normal(ks[5], (DEPTH, D_MODEL, D_IN), f32) * D_MODEL ** -0.5
    qk_g = 1.0 + 0.02 * jax.random.normal(ks[6], (DEPTH, 4, HEAD_DIM), f32)
    out_g = 1.0 + 0.02 * jax.random.normal(ks[7], (DEPTH, D_MIX), f32)
    w_out = jax.random.normal(ks[8], (DEPTH, D_MIX, D_MODEL), f32) * D_MIX ** -0.5
    ffn_w1 = jax.random.normal(ks[9], (DEPTH, 2, D_MODEL, D_FF), f32) * D_MODEL ** -0.5
    ffn_w3 = jax.random.normal(ks[10], (DEPTH, 2, D_MODEL, D_FF), f32) * D_MODEL ** -0.5
    ffn_w2 = jax.random.normal(ks[11], (DEPTH, 2, D_FF, D_MODEL), f32) * D_FF ** -0.5
    return {"x": x, "c": c, "w_ada": w_ada, "b_ada": b_ada, "norm_g": norm_g, "w_in": w_in,
            "qk_g": qk_g, "out_g": out_g, "w_out": w_out, "ffn_w1": ffn_w1,
            "ffn_w3": ffn_w3, "ffn_w2": ffn_w2}

def second_block(x, c, w_ada, b_ada, norm_g, w_in, qk_g, out_g, w_out, ffn_w1, ffn_w3, ffn_w2):
    B, S, _ = x.shape
    cos, sin = rope_tables_2(S)
    split_points = [int(p) for p in np.cumsum(SPLIT_SIZES)[:-1]]
    silu_c = jax.nn.silu(c)
    for layer in range(DEPTH):
        mod = silu_c @ w_ada[layer] + b_ada[layer]
        sh1, sc1, g1, sh2, sc2, g2, sh3, sc3, g3 = [m[:, None, :] for m in jnp.split(mod, N_MOD, axis=-1)]

        h = modulate(rmsnorm(x, norm_g[layer, 0]), sh1, sc1)
        x = x + 0.5 * g1 * swiglu_2(h, ffn_w1[layer, 0], ffn_w3[layer, 0], ffn_w2[layer, 0])

        h = modulate(rmsnorm(x, norm_g[layer, 1]), sh2, sc2)
        proj = h @ w_in[layer]
        (qa, ka, va, qb, kb, vb, qi, ki, wi, qc, kc, vc) = jnp.split(proj, split_points, axis=-1)
        heads = lambda t, n: t.reshape(B, S, n, HEAD_DIM)
        qa = apply_partial_rope(rmsnorm(heads(qa, N_HEADS_A), qk_g[layer, 0]), cos, sin)
        ka = apply_partial_rope(rmsnorm(heads(ka, N_HEADS_A), qk_g[layer, 1]), cos, sin)
        qb = apply_partial_rope(rmsnorm(heads(qb, N_HEADS_B), qk_g[layer, 2]), cos, sin)
        kb = apply_partial_rope(rmsnorm(heads(kb, N_HEADS_B), qk_g[layer, 3]), cos, sin)
        qi = apply_partial_rope(qi.reshape(B, S, IDX_HEADS, IDX_DIM), cos, sin)
        ki = apply_partial_rope(ki[:, :, None, :], cos, sin)[:, :, 0, :]

        oa = moba_attention(qa, ka, heads(va, N_HEADS_A))
        ob = dsa_attention(qb, kb, heads(vb, N_HEADS_B), qi, ki, wi)
        oc = stick_breaking_attention(heads(qc, N_HEADS_C), heads(kc, N_HEADS_C), heads(vc, N_HEADS_C))

        o = jnp.concatenate([oa, ob, oc], axis=2)
        o = (_rms(o).reshape(B, S, D_MIX) * out_g[layer].astype(jnp.float32)).astype(x.dtype)
        x = x + g2 * (o @ w_out[layer])

        h = modulate(rmsnorm(x, norm_g[layer, 2]), sh3, sc3)
        x = x + 0.5 * g3 * swiglu_2(h, ffn_w1[layer, 1], ffn_w3[layer, 1], ffn_w2[layer, 1])
    return x


def setup_inputs(seed=0):
    out = dict(first_inputs(seed))
    for name, value in second_inputs(seed + 1).items():
        if name != "x":
            out[name + "_2"] = value
    return out


def reference(
    x, mem, positions, ffn1_norm, ffn1_w_gu, ffn1_w_down, mix_norm, w_in, hgrn_lower_bounds,
    hgrn_head_norm, w_att_branch, w_hgrn_branch, w_mix_out, xattn_norm, mem_norm, xattn_wq,
    xattn_wkv, xattn_wo, ffn2_norm, ffn2_w_gu, ffn2_w_down, final_norm, c_2, w_ada_2, b_ada_2,
    norm_g_2, w_in_2, qk_g_2, out_g_2, w_out_2, ffn_w1_2, ffn_w3_2, ffn_w2_2,
):
    x = first_block(
        x, mem, positions, ffn1_norm, ffn1_w_gu, ffn1_w_down, mix_norm, w_in, hgrn_lower_bounds,
        hgrn_head_norm, w_att_branch, w_hgrn_branch, w_mix_out, xattn_norm, mem_norm, xattn_wq,
        xattn_wkv, xattn_wo, ffn2_norm, ffn2_w_gu, ffn2_w_down, final_norm,
    )
    return second_block(
        x, c_2, w_ada_2, b_ada_2, norm_g_2, w_in_2, qk_g_2, out_g_2, w_out_2, ffn_w1_2,
        ffn_w3_2, ffn_w2_2,
    )


_drawn_inputs = setup_inputs


def setup_inputs(seed=0):
    import zlib

    import numpy as np

    out = dict(_drawn_inputs(seed))
    spreads = {}
    factors = {'ffn1_norm': 3.086,
     'hgrn_head_norm': 4.608,
     'xattn_norm': 8.0,
     'mem_norm': 7.478,
     'ffn2_norm': 3.87,
     'qk_g_2': 8.0,
     'out_g_2': 4.01}
    for name, (base, spread) in spreads.items():
        noise = np.random.default_rng([zlib.crc32(name.encode()), seed]).standard_normal(out[name].shape)
        drawn = base * np.exp(spread * noise) if base else spread * noise
        out[name] = __import__('jax').numpy.asarray(drawn.astype(out[name].dtype))
    for name, factor in factors.items():
        out[name] = (out[name] * factor).astype(out[name].dtype)
    return out
```

```python
from contextlib import ExitStack

import numpy as np

import concourse.bass as bass
from concourse import mybir

F32 = mybir.dt.float32
F32R = mybir.dt.float32r
BF16 = mybir.dt.bfloat16
I32 = mybir.dt.int32
U8 = mybir.dt.uint8
ACT = mybir.ActivationFunctionType
ALU = mybir.AluOpType
AX = mybir.AxisListType

P = 128
T = 256
D = 1024
KD = D // P
DEPTH = 2
D_FF = 2816
CHUNKS = D_FF // T
EPS = 1e-6
GROUPS = ((128, 1), (512, 4), (2048, 16))
NG = len(GROUPS)
HEADS = 4
DH = 128
HG = 8
XHD = 256
NEG = -1e30
PICKED = -3e38
RING = 6
SPLITS = 3
TILE = 2048
FFN_TILES = 3 * CHUNKS
TWO_PI = 2 * np.pi

FFN_A = 0
MIX = FFN_A + FFN_TILES
M_F, M_Q, M_I = MIX, MIX + 4, MIX + 8
M_QK, M_V = MIX + 12, MIX + 24
M_OG, M_GA, M_GB = MIX + 30, MIX + 34, MIX + 38
M_YB, M_YA = MIX + 42, MIX + 46
M_KV0 = M_YA + 2
M_OUT = M_KV0 + 2
M_KV1 = M_OUT + 4
X_Q = M_KV1 + 6
X_O = X_Q + 4
FFN_B = X_O + 4
TILES_1 = FFN_B + FFN_TILES

HD = 64
HA, HB, HC = 4, 4, 8
IDX = 8
ROPE_DIM = 16
TOPK = min(256, T // 4)
ADA = 0
N_FRONT = KD
N_MID = 3 * KD // 2
N_LATE = 2 * KD
FFN_C = ADA + N_FRONT
ADA_MID = FFN_C + FFN_TILES
Z_QI = ADA_MID + N_MID
Z_KI = Z_QI + 2
Z_B = Z_KI + 1
Z_A = Z_B + 2
Z_V = Z_A + 2
Z_C = Z_V + 4
Z_LATE = Z_C + 4
Z_O = Z_LATE + N_LATE
FFN_D = Z_O + 4
TILES_2 = FFN_D + FFN_TILES

USES_1 = [(TILES_1 - j + RING - 1) // RING for j in range(RING)]
USES_2 = [(TILES_2 - j + RING - 1) // RING for j in range(RING)]

V1_FFN1, V1_MIX, V1_HEAD, V1_X, V1_MEM, V1_FFN2 = (KD * i for i in range(6))
V1_W = 6 * KD
V2_NORM, V2_OUT, V2_QK, V2_ADA = 0, 3 * KD, 4 * KD, 4 * KD + 4
V2_W = V2_ADA + 72
VEC_1 = 0
VEC_2 = VEC_1 + DEPTH * V1_W
VEC_LB = VEC_2 + DEPTH * V2_W
VEC_FIN = VEC_LB + DEPTH * KD
VEC_C = VEC_FIN + KD
VEC_INV = VEC_C + KD
VEC_W = VEC_INV + 1

C_ID, C_ONE, C_BD, C_R1, C_R2, C_TRI = (P * i for i in range(6))
C_OWN = 6 * P
C_M1 = C_OWN
C_M2 = C_OWN
C_M3 = C_M2 + 3 * P
C_COS = C_M3 + 3 * P
C_SIN = C_COS + T
C_W = C_SIN + T
C_NEXT = C_W - C_OWN
LEVELS = 8
RUN = 64


class Chain:

    def __init__(self, eng, sem):
        self.eng, self.sem, self.n = eng, sem, 0

    def __call__(self, ins):
        self.n += 1
        ins.then_inc(self.sem, 1)
        self.eng.wait_ge(self.sem, self.n)


def program(nc, x_t, mem_t, pos, stream, vec, con, lmask, out):
    with ExitStack() as ctx:
        def sb(name, shape, dt=F32):
            return ctx.enter_context(nc.sbuf_tensor(name, shape, dt))

        def sem(name):
            return ctx.enter_context(nc.semaphore(name))

        ring = sb("ring", [P, RING, TILE])
        x = sb("x", [P, KD, T])
        h = sb("h", [P, KD, T])
        mem = sb("mem", [P, KD, T])
        ffn_x_at = nc.sbuf_base
        qk = sb("qk", [P, 24, T])
        val = sb("val", [P, 2, NG * HEADS * DH])
        ffn_w_at = nc.sbuf_base
        hq = sb("hq", [P, KD, T])
        hk = sb("hk", [P, KD, T])
        hb = sb("hb", [P, KD, T])
        hi = sb("hi", [P, 2, D])
        a_hg = sb("a_hg", [P, HG, 3, P])
        att = sb("att", [P, HEADS, T])
        assert nc.sbuf_base - ffn_w_at == SPLITS * 2 * TILE * 4
        w_hi = nc.alloc_sbuf_tensor_at("w_hi", [P, SPLITS, TILE], F32R, offset=ffn_w_at)
        w_lo = nc.alloc_sbuf_tensor_at("w_lo", [P, SPLITS, TILE], F32R, offset=ffn_w_at + SPLITS * TILE * 4)
        h_hi = nc.alloc_sbuf_tensor_at("h_hi", [P, KD, T], F32R, offset=ffn_x_at)
        h_lo = nc.alloc_sbuf_tensor_at("h_lo", [P, KD, T], F32R, offset=ffn_x_at + KD * T * 4)
        g_hi = nc.alloc_sbuf_tensor_at("g_hi", [P, 2, 512], F32R, offset=ffn_x_at + 2 * KD * T * 4)
        g_lo = nc.alloc_sbuf_tensor_at("g_lo", [P, 2, 512], F32R, offset=ffn_x_at + 2 * KD * T * 4 + 4096)
        e_buf = [sb("e0", [P, KD, T]), sb("e1", [P, KD, T])]
        prob = [sb("prob0", [P, 9 * P]), sb("prob1", [P, 9 * P])]
        prob_t = sb("prob_t", [P, NG, 3 * P])
        con_sb = sb("con_sb", [P, C_W])
        vec_sb = sb("vec_sb", [P, VEC_W])
        lm = sb("lm", [P, LEVELS, P], U8)
        cos1 = sb("cos1", [P, T])
        sin1 = sb("sin1", [P, T])
        rope_a = sb("rope_a", [P, 2, T])
        rope_b = sb("rope_b", [P, 2, T])
        rstd = sb("rstd", [P, T])
        var = sb("var", [P, T])
        v_now = sb("v_now", [P, V2_W])
        mod = sb("mod", [P, 72])
        lb = sb("lb", [P, DEPTH, KD])
        lb_now = sb("lb_now", [P, 2, KD])
        small = sb("small", [P, 16])
        small2 = sb("small2", [P, 2 * IDX])
        one = sb("one", [P, 1])
        eps = sb("eps", [P, 1])
        silu_c = sb("silu_c", [P, KD])
        zeros = sb("zeros", [P, 512], BF16)
        pos_i = sb("pos_i", [P, T], I32)
        g_buf = [prob[0][:, 0:512], prob[1][:, 0:512]]
        ps = ctx.enter_context(nc.psum_tensor("ps", [P, 8, 512], F32))

        def C(at, n):
            return con_sb[:, at:at + n]

        ident, ones = C(C_ID, P), C(C_ONE, P)

        loaded = [sem(f"slot_loaded{j}") for j in range(RING)]
        first = sem("tile_done")
        s = {"tile_done": first}
        for name in (
            "dve_chain", "act_chain", "pool_chain", "w_hi_ready", "w_lo_ready", "silu_done", "hidden_step", "prod_done", "x_ready", "sq_ready",
            "ss_ready", "var_ready", "rstd_ready", "h_ready", "evac_done", "forget_ready", "log_ready",
            "cumsum_ready", "decay_arg", "decay_exp", "e_ready", "level_done", "level_used", "a_zeroed", "rot_done",
            "rot_scaled", "rope_done", "o_done", "o_copied", "o_ss", "o_var", "o_rstd", "o_ready", "scores_done",
            "scores_read", "max_ready", "exp_ready", "probs_ready", "pt_done", "pt_ready", "pv_done",
            "att_ready", "yb_used", "ya_used", "merged", "mem_ready", "store", "load", "vec_ready",
            "mod_ready", "head_sq", "head_ss", "head_var", "head_rs", "head_ready", "ki_ready",
            "logit_done", "relu_ready", "relu_used", "z_done", "zm_ready", "soft_ready",
            "l_ready", "cum_done", "arg_ready", "a_ready", "wi_ready", "last",
        ):
            s[name] = sem(name)
        nums = [v.num for v in s.values()]
        layer_sems = range(min(nums), max(nums) + 1)
        S = type("S", (), s)


        def slot_wait(pe, l, block, p, m=0):
            j = p % RING
            if block == 1:
                before = l * (16 * USES_1[j]) + 16 * (p // RING + 1)
            else:
                before = l * (16 * USES_2[j]) + 16 * (DEPTH * USES_1[j] + p // RING + 1)
            pe.wait_ge(loaded[j], before + m * 16 if not isinstance(m, int) else before)

        def block_w(p, k, n):
            return ring[:, p % RING, k * T + n * P:k * T + (n + 1) * P]

        def project(pe, l, block, p, bank, src, m=0, start=True):
            slot_wait(pe, l, block, p, m)
            for n in range(2):
                for k in range(KD):
                    mm = nc.tensor.matmul(ps[:, bank, n * T:(n + 1) * T], block_w(p, k, n), src[:, k, :],
                                          start=(k == 0), stop=(k == KD - 1))
            mm.then_inc(S.tile_done, 1)

        def project_tok(pe, l, block, p, bank, src):
            slot_wait(pe, l, block, p)
            for t in range(2):
                for k in range(KD):
                    mm = nc.tensor.matmul(ps[:, bank, t * T:(t + 1) * T], src[:, k, t * P:(t + 1) * P],
                                          ring[:, p % RING, k * T:(k + 1) * T],
                                          start=(k == 0), stop=(k == KD - 1))
            mm.then_inc(S.tile_done, 1)

        def stream_in(sp, l, tiles, base, last_layer):
            full = tiles // RING
            with sp.Fori(1, full) as g:
                for j in range(RING):
                    sp.wait_ge(S.tile_done, g * RING + (j - RING + 1))
                    sp.dma_start(ring[:, j, :], tile_at(g * RING + l * tiles + (base + j))).then_inc(loaded[j], 16)
            for p in range(full * RING, tiles):
                sp.wait_ge(S.tile_done, p - RING + 1)
                sp.dma_start(ring[:, p % RING, :], tile_at(l * tiles + (base + p))).then_inc(loaded[p % RING], 16)

            def ahead(l):
                for j in range(RING):
                    last = (tiles - 1 - j) // RING * RING + j
                    sp.wait_ge(S.tile_done, last + 1)
                    sp.dma_start(ring[:, j, :], tile_at(l * tiles + (base + tiles + j))).then_inc(loaded[j], 16)
            if last_layer:
                assert DEPTH == 2
                with sp.If(l < DEPTH - 1):
                    ahead(0)
            else:
                ahead(l)

        def tile_at(i):
            return stream[bass.ds(i, 1)].rearrange("o p n -> p (o n)")

        def norm_act(act, chain, n, x_count, sq, src=x, between=None):
            for half in range(2):
                if x_count:
                    act.wait_ge(S.x_ready, x_count)
                nc.scalar.activation(sq[:, 4 * half:4 * half + 4, :], src[:, 4 * half:4 * half + 4, :],
                                     ACT.Square).then_inc(S.sq_ready, 1)
            if between:
                between()
            act.wait_ge(S.var_ready, n + 1)
            chain(nc.scalar.activation(rstd[:], var[:], ACT.Ln))
            nc.scalar.activation(rstd[:], rstd[:], ACT.Exp, scale=-0.5).then_inc(S.rstd_ready, 1)

        def norm_pe(pe, n, sq):
            for k in range(KD):
                if k % 4 == 0:
                    pe.wait_ge(S.sq_ready, 2 * n + k // 4 + 1)
                mm = nc.tensor.matmul(ps[:, 0, 0:T], ones, sq[:, k, :], start=(k == 0), stop=(k == KD - 1))
            mm.then_inc(S.ss_ready, 1)

        def refine(chain, r, v):
            chain(nc.vector.scalar_tensor_tensor(out=v, in0=r, scalar=-0.5, in1=v, op0=ALU.mult, op1=ALU.mult))
            chain(nc.vector.tensor_tensor(v, v, r, ALU.mult))
            chain(nc.vector.scalar_tensor_tensor(out=r, in0=v, scalar=1.5, in1=r, op0=ALU.add, op1=ALU.mult))

        def rstd_dve(dve, chain, n):
            dve.wait_ge(S.ss_ready, n + 1)
            nc.vector.tensor_scalar(var[:], ps[:, 0, 0:T], 1.0 / D, EPS, ALU.mult, ALU.add).then_inc(S.var_ready, 1)
            dve.wait_ge(S.rstd_ready, n + 1)
            refine(chain, rstd[:], var[:])

        def norm_dve(dve, chain, n, x_count, gain, shift=None, src=x, dst=h, split=False, stats=True, between=None):
            if x_count:
                dve.wait_ge(S.x_ready, x_count)
            for k in range(KD):
                ins = nc.vector.tensor_scalar(dst[:, k, :], src[:, k, :], gain[:, k:k + 1], None, ALU.mult)
            chain(ins)
            if between:
                between()
            if stats:
                rstd_dve(dve, chain, n)
            for half in range(2):
                part = dst[:, 4 * half:4 * half + 4, :]
                ins = nc.vector.tensor_tensor(part, part, rstd[:].unsqueeze(1).broadcast_to([P, 4, T]), ALU.mult)
                if shift is not None:
                    chain(ins)
                    for k in range(4 * half, 4 * half + 4):
                        ins = nc.vector.tensor_scalar(dst[:, k, :], dst[:, k, :], shift[:, k:k + 1], None, ALU.add)
                if split:
                    chain(ins)
                    hi_, lo = (b[:, 4 * half:4 * half + 4, :] for b in (h_hi, h_lo))
                    chain(nc.vector.tensor_copy(hi_, part))
                    ins = nc.vector.tensor_tensor(lo, part, hi_.bitcast(F32), ALU.subtract)
                ins.then_inc(S.h_ready, 1)

        def triple(out, hi_w, lo_w, hi_x, lo_x, start, stop, group=False):
            for n, (a, b) in enumerate(((hi_w, hi_x), (hi_w, lo_x), (lo_w, hi_x))):
                mm = nc.tensor.matmul(out, a, b, start=start and n == 0, stop=stop and n == 2,
                                      skip_group_check=group)
            return mm

        def ffn_pe(pe, p0, f, n):
            def split_wait(t, m):
                pe.wait_ge(S.w_lo_ready, count(f, t, m))

            def gate_up(i, t, bank, m, inputs=None):
                for which, done in ((0, S.silu_done), (1, S.prod_done)):
                    pe.wait_ge(done, i + (CHUNKS * f + 1))
                    split_wait(t + which, m)
                    slot = (t + which) % SPLITS
                    for a in range(2):
                        for k in range(KD):
                            if inputs and which == 0 and a == 0 and k == KD // 2:
                                pe.wait_ge(S.h_ready, inputs)
                            w = slice(k * T + a * P, k * T + (a + 1) * P)
                            mm = triple(ps[:, 2 * which + bank, a * T:(a + 1) * T], w_hi[:, slot, w],
                                        w_lo[:, slot, w], h_hi[:, k, :], h_lo[:, k, :], k == 0, k == KD - 1)
                    mm.then_inc(S.tile_done, 1)

            def down(i, t, buf, m):
                pe.wait_ge(S.prod_done, i + (CHUNKS * f + 3))
                split_wait(t, m)
                for k in range(2):
                    for d in range(KD):
                        w = slice(k * D + d * P, k * D + (d + 1) * P)
                        xs = slice(k * T, (k + 1) * T)
                        mm = triple(ps[:, 4 + d // 2, (d % 2) * T:(d % 2 + 1) * T], w_hi[:, t % SPLITS, w],
                                    w_lo[:, t % SPLITS, w], g_hi[:, buf, xs], g_lo[:, buf, xs], False, True, True)
                mm.then_inc(S.tile_done, 1)

            for b in range(4):
                nc.tensor.matmul(ps[:, 4 + b, :], zeros[:, 0:P], zeros[:], start=True, stop=True)
            pe.wait_ge(S.h_ready, 2 * n + 1)
            gate_up(0, 0, 0, 0, inputs=2 * n + 2)
            with pe.Fori(0, CHUNKS // 2) as m:
                for b in range(2):
                    t = 2 + 3 * b
                    gate_up(2 * m + (1 + b), t, (1 + b) % 2, m)
                    down(2 * m + b, t + 2, b, m)
            down(CHUNKS - 1, FFN_TILES - 1, (CHUNKS - 1) % 2, 0)

        def count(f, t, m):
            c = FFN_TILES * f + t + 1
            return c if isinstance(m, int) else m * RING + c

        def done(p0, t, m):
            return p0 + t + 1 if isinstance(m, int) else m * RING + (p0 + t + 1)

        def first_high(act, l, block, p0, tiles=range(SPLITS)):
            for t in tiles:
                slot_wait(act, l, block, p0 + t)
                nc.scalar.activation(w_hi[:, t, :], ring[:, (p0 + t) % RING, :], ACT.Copy).then_inc(S.w_hi_ready, 1)

        def ffn_act(act, l, block, p0, f):
            def split(t, m):
                if isinstance(m, int) and t >= FFN_TILES:
                    return
                act.wait_ge(S.tile_done, done(p0, t - SPLITS, m))
                slot_wait(act, l, block, p0 + t, m)
                nc.scalar.activation(w_hi[:, t % SPLITS, :], ring[:, (p0 + t) % RING, :],
                                     ACT.Copy).then_inc(S.w_hi_ready, 1)

            def silu(t, b, m):
                act.wait_ge(S.tile_done, done(p0, t, m))
                nc.scalar.activation(g_buf[b], ps[:, b, :], ACT.Silu).then_inc(S.silu_done, 1)

            silu(0, 0, 0)
            split(SPLITS, 0)
            split(SPLITS + 1, 0)
            with act.Fori(0, CHUNKS // 2 - 1) as m:
                for b in range(2):
                    t = 2 + 3 * b
                    silu(t, (1 + b) % 2, m)
                    for i in range(3):
                        split(t + SPLITS + i, m)
            m = CHUNKS // 2 - 1
            for b in range(2):
                t = RING * m + 2 + 3 * b
                silu(t, (1 + b) % 2, 0)
                for i in range(3):
                    split(t + SPLITS + i, 0)

        def low_split(dve, p0, f, t, m):
            if isinstance(m, int) and t >= FFN_TILES:
                return
            dve.wait_ge(S.w_hi_ready, count(f, t, m))
            nc.vector.tensor_tensor(w_lo[:, t % SPLITS, :], ring[:, (p0 + t) % RING, :],
                                    w_hi[:, t % SPLITS, :].bitcast(F32), ALU.subtract).then_inc(S.w_lo_ready, 1)

        def first_low(dve, p0, f, tiles):
            for t in tiles:
                low_split(dve, p0, f, t, 0)

        def ffn_dve(dve, p0, f, split_before):
            def split(t, m):
                low_split(dve, p0, f, t, m)

            def gated(i, t, b, m):
                dve.wait_ge(S.silu_done, i + (CHUNKS * f + 3))
                dve.wait_ge(S.tile_done, done(p0, t, m))
                steps = 2 * (CHUNKS * f) + 1
                nc.vector.tensor_tensor(g_buf[b], g_buf[b], ps[:, 2 + b, :], ALU.mult).then_inc(S.hidden_step, 1)
                dve.wait_ge(S.hidden_step, i * 2 + steps)
                nc.vector.tensor_copy(g_hi[:, b, :], g_buf[b]).then_inc(S.hidden_step, 1)
                dve.wait_ge(S.hidden_step, i * 2 + (steps + 1))
                nc.vector.tensor_tensor(g_lo[:, b, :], g_buf[b], g_hi[:, b, :].bitcast(F32),
                                        ALU.subtract).then_inc(S.prod_done, 1)

            for t in range(split_before, SPLITS):
                split(t, 0)
            split(SPLITS, 0)
            gated(0, 1, 0, 0)
            split(SPLITS + 1, 0)
            with dve.Fori(0, CHUNKS // 2 - 1) as m:
                for b in range(2):
                    t = 2 + 3 * b
                    split(t + SPLITS, m)
                    gated(2 * m + (1 + b), t + 1, (1 + b) % 2, m)
                    split(t + SPLITS + 1, m)
                    split(t + SPLITS + 2, m)
            m = CHUNKS // 2 - 1
            for b in range(2):
                t = RING * m + 2 + 3 * b
                split(t + SPLITS, 0)
                gated(2 * m + (1 + b), t + 1, (1 + b) % 2, 0)
                split(t + SPLITS + 1, 0)
                split(t + SPLITS + 2, 0)

        def residual(dve, p_last, bank, scale):
            for b in range(4):
                dve.wait_ge(S.tile_done, p_last(b) + 1)
                if isinstance(scale, float):
                    part = x[:, 2 * b:2 * b + 2, :].rearrange("p k t -> p (k t)")
                    nc.vector.scalar_tensor_tensor(out=part, in0=ps[:, bank + b, :], scalar=scale, in1=part,
                                                   op0=ALU.mult, op1=ALU.add).then_inc(S.x_ready, 1)
                else:
                    for k in (2 * b, 2 * b + 1):
                        ins = nc.vector.scalar_tensor_tensor(
                            out=x[:, k, :], in0=ps[:, bank + b, (k % 2) * T:(k % 2 + 1) * T],
                            scalar=scale[:, k:k + 1], in1=x[:, k, :], op0=ALU.mult, op1=ALU.add)
                    ins.then_inc(S.x_ready, 1)

        with nc.Block() as block:
            @block.sync
            def _(sp):
                sp.dma_start(con_sb[:], con[:, 0:C_W]).then_inc(S.load, 16)
                sp.dma_start(vec_sb[:], vec).then_inc(S.load, 16)
                sp.dma_start(pos_i[:], pos.broadcast_to([P, T])).then_inc(S.load, 16)
                sp.dma_start(e_buf[1][:].rearrange("p k t -> p (k t)")[:, 0:LEVELS * P], lmask).then_inc(S.load, 16)
                sp.dma_start(mem[:], mem_t.rearrange("(k p) t -> p k t", p=P)).then_inc(S.load, 16)
                sp.dma_start(x[:], x_t.rearrange("(k p) t -> p k t", p=P)).then_inc(S.load, 16)
                for j in range(RING):
                    sp.dma_start(ring[:, j, :], stream[j]).then_inc(loaded[j], 16)
                sp.wait_ge(S.load, 96)

            @block.gpsimd
            def _(pool):
                nc.gpsimd.memset(zeros[:], 0.0)
                nc.gpsimd.memset(one[:], 1.0)
                nc.gpsimd.memset(eps[:], EPS).then_inc(S.vec_ready, 1)

            @block.tensor
            def _(pe):
                norm_pe(pe, 0, e_buf[0])

            @block.scalar
            def _(act):
                chain = Chain(act, S.act_chain)
                act.wait_ge(S.load, 96)
                act.wait_ge(S.vec_ready, 1)
                norm_act(act, chain, 0, 0, e_buf[0], mem)
                act.wait_ge(S.decay_arg, 1)
                nc.scalar.activation(lb[:], lb[:], ACT.Exp).then_inc(S.decay_exp, 1)
                act.wait_ge(S.rot_scaled, 1)
                nc.scalar.activation(sin1[:], sin1[:], ACT.Sin)
                nc.scalar.activation(cos1[:], cos1[:], ACT.Sin)

            @block.vector
            def _(dve):
                chain = Chain(dve, S.dve_chain)
                dve.wait_ge(S.load, 96)
                nc.vector.tensor_copy(lm[:].rearrange("p a b -> p (a b)"),
                                      e_buf[1][:].rearrange("p k t -> p (k t)")[:, 0:LEVELS * P])
                rstd_dve(dve, chain, 0)
                nc.vector.tensor_tensor(mem[:], mem[:], rstd[:].unsqueeze(1).broadcast_to([P, KD, T]), ALU.mult)
                lbv = vec_sb[:, VEC_LB:VEC_LB + DEPTH * KD].rearrange("p (l k) -> p l k", l=DEPTH)
                top = small[:, 0:KD]
                chain(nc.vector.tensor_tensor(top, lbv[:, 0, :], lbv[:, 1, :], ALU.max))
                nc.vector.tensor_tensor(lb[:], lbv, top.unsqueeze(1).broadcast_to([P, DEPTH, KD]),
                                        ALU.subtract).then_inc(S.decay_arg, 1)
                dve.wait_ge(S.decay_exp, 1)
                chain(nc.vector.tensor_tensor(top, lb[:, 0, :], lb[:, 1, :], ALU.add))
                chain(nc.vector.reciprocal(top, top))
                chain(nc.vector.tensor_tensor(lb[:], lb[:], top.unsqueeze(1).broadcast_to([P, DEPTH, KD]), ALU.mult))
                chain(nc.vector.tensor_tensor(lb[:, 1, :], lb[:, 0, :], lb[:, 1, :], ALU.add))
                chain(nc.vector.tensor_tensor(lb[:, 1, :], lb[:, 1, :], lb[:, 0, :], ALU.subtract))
                chain(nc.vector.tensor_tensor(lb[:, 0, :], lb[:, 0, :], lb[:, 0, :], ALU.subtract))
                ang, turn = rope_a[:, 0, :], rope_b[:, 0, :]
                chain(nc.vector.tensor_copy(ang, pos_i[:]))
                chain(nc.vector.tensor_scalar(ang, ang, vec_sb[:, VEC_INV:VEC_INV + 1], None, ALU.mult))
                whole = 1.5 * 2.0 ** 23
                c1 = 6.28125
                c2 = float(np.float32(np.round((TWO_PI - c1) * 2.0 ** 21) / 2.0 ** 21))
                c3 = TWO_PI - c1 - c2
                for table, quarter in ((sin1, 0.0), (cos1, 0.25)):
                    chain(nc.vector.tensor_scalar(turn, ang, 1 / TWO_PI, quarter, ALU.mult, ALU.add))
                    chain(nc.vector.tensor_scalar(turn, turn, whole, None, ALU.add))
                    chain(nc.vector.tensor_scalar(turn, turn, whole, None, ALU.subtract))
                    chain(nc.vector.scalar_tensor_tensor(out=table[:], in0=turn, scalar=-c1, in1=ang,
                                                         op0=ALU.mult, op1=ALU.add))
                    for c in (c2, c3):
                        chain(nc.vector.scalar_tensor_tensor(out=table[:], in0=turn, scalar=-c, in1=table[:],
                                                             op0=ALU.mult, op1=ALU.add))
                    chain(nc.vector.tensor_scalar(table[:], table[:], quarter * TWO_PI, None, ALU.add))
                    pi = float(np.nextafter(np.float32(np.pi), np.float32(0)))
                    chain(nc.vector.tensor_scalar(table[:], table[:], pi, -pi, ALU.min, ALU.max))
                nc.vector.memset(small[:, 15:16], 0.0).then_inc(S.rot_scaled, 1)
        nc.all_engine_barrier(sems_to_clear=layer_sems)

        levels = [P >> i for i in range(LEVELS)]
        b_flat = hb[:].rearrange("p k t -> p (k t)")
        hq_flat = hq[:].rearrange("p k t -> p (k t)")
        hi_flat = hi[:].rearrange("p a v -> p (a v)")

        def halves(buf, half):
            v = buf[:].rearrange("p k (g two c) -> p (k g) two c", two=2, c=half)
            return v[:, :, 0, :], v[:, :, 1, :]

        def one_pe(pe, l):
            norm_pe(pe, 0, e_buf[0])
            ffn_pe(pe, FFN_A, 0, 0)
            norm_wait = 4
            pe.wait_ge(S.x_ready, norm_wait)
            norm_pe(pe, 1, e_buf[0])
            pe.wait_ge(S.h_ready, 4)
            for n in range(12):
                if n >= 3:
                    pe.wait_ge(S.evac_done, n - 2)
                (project_tok if n >= 8 else project)(pe, l, 1, MIX + n, n % 3, h)

            def rotate(n):
                pe.wait_ge(S.evac_done, 12 + n + 1)
                if n >= 1:
                    pe.wait_ge(S.rot_scaled, n)
                nc.tensor.matmul(ps[:, 3, :], C(C_R1, P), qk[:, 2 * n:2 * n + 2, :].rearrange("p k t -> p (k t)"),
                                 start=True, stop=True).then_inc(S.rot_done, 1)

            def level(i):
                if i < LEVELS:
                    pe.wait_ge(S.e_ready, i + 1)
                sta, mov = (e_buf[i % 2], e_buf[i % 2]) if i < LEVELS else (hk, hq)
                for g in range(2):
                    if i >= 1:
                        pe.wait_ge(S.level_used, 2 * (i - 1) + g + 1)
                    for hd in range(4 * g, 4 * g + 4):
                        j = hd % 4
                        if i == 0:
                            mm = nc.tensor.matmul(ps[:, 4 + 2 * g, j * P:(j + 1) * P], sta[:, hd, 0:P],
                                                  mov[:, hd, P:T], start=True, stop=True)
                            continue
                        for t in range(2):
                            at = (j % 2) * T + t * P
                            mm = nc.tensor.matmul(ps[:, 4 + 2 * g + j // 2, at:at + P],
                                                  sta[:, hd, t * P:(t + 1) * P], mov[:, hd, t * P:(t + 1) * P],
                                                  start=True, stop=True)
                    mm.then_inc(S.level_done, 1)

            for i in range(LEVELS + 1):
                for n in (2 * i, 2 * i + 1):
                    pe.wait_ge(S.evac_done, 12 + n - 2)
                    (project if n < 12 else project_tok)(pe, l, 1, M_QK + n, (12 + n) % 3, h)
                    if 1 <= n <= 12:
                        rotate(n - 1)
                if i == LEVELS:
                    pe.wait_ge(S.cumsum_ready, 1)
                level(i)

            def gate_tile(n):
                pe.wait_ge(S.evac_done, 30 + n - 1 if n >= 2 else 30)
                project(pe, l, 1, M_OG + n, n % 2, h)

            gate_tile(0)
            gate_tile(1)
            for hd in range(HG):
                if hd % 4 == 0:
                    pe.wait_ge(S.level_used, 2 * LEVELS + hd // 4 + 1)
                o = ps[:, 4 + hd // 2, (hd % 2) * T:(hd % 2 + 1) * T]
                v = slice(hd * P, (hd + 1) * P)
                nc.tensor.matmul(o, hi[:, 0, v], a_hg[:, hd, 0:2, :].rearrange("p a t -> p (a t)"),
                                 start=True, stop=False, skip_group_check=True)
                mm = nc.tensor.matmul(o[:, P:T], hi[:, 1, v], a_hg[:, hd, 2, :], start=False, stop=True,
                                      skip_group_check=True)
                if hd % 4 == 3:
                    mm.then_inc(S.o_done, 1)
            gate_tile(2)
            gate_tile(3)
            for b in range(4):
                if b % 2 == 0:
                    pe.wait_ge(S.o_copied, b // 2 + 1)
                mm = nc.tensor.matmul(ps[:, 4 + b, :], ones, hq[:, 2 * b:2 * b + 2, :].rearrange("p k t -> p (k t)"),
                                      start=True, stop=True)
            mm.then_inc(S.o_ss, 1)
            gate_tile(4)

            def scores(hd):
                if hd == 0:
                    pe.wait_ge(S.rope_done, 12)
                    pe.wait_ge(S.o_rstd, 1)
                else:
                    pe.wait_ge(S.scores_read, 2 * hd)
                    pe.wait_ge(S.pt_ready, hd)
                for g in range(NG):
                    q, k = qk[:, g * HEADS + hd, :], qk[:, (NG + g) * HEADS + hd, :]
                    nc.tensor.matmul(ps[:, 4, g * P:(g + 1) * P], q[:, 0:P], k[:, 0:P], start=True, stop=True)
                    mm = nc.tensor.matmul(ps[:, 5 + g // 2, (g % 2) * T:(g % 2 + 1) * T], q[:, P:T], k,
                                          start=True, stop=True)
                mm.then_inc(S.scores_done, 1)

            def flip(hd):
                pe.wait_ge(S.probs_ready, hd + 1)
                if hd >= 1:
                    pe.wait_ge(S.pt_ready, hd)
                p = prob[hd % 2]
                for g in range(NG):
                    for c, at in enumerate((g * P, 3 * P + g * T, 3 * P + g * T + P)):
                        mm = nc.tensor.transpose(ps[:, 2 + g, c * P:(c + 1) * P], p[:, at:at + P], ident)
                mm.then_inc(S.pt_done, 1)

            def weigh(hd):
                pe.wait_ge(S.pt_ready, hd + 1)
                if hd >= 2:
                    pe.wait_ge(S.att_ready, hd - 1)
                o = ps[:, 7, (hd % 2) * T:(hd % 2 + 1) * T]
                for g in range(NG):
                    v = slice((g * HEADS + hd) * DH, (g * HEADS + hd + 1) * DH)
                    nc.tensor.matmul(o, val[:, 0, v], prob_t[:, g, 0:T], start=(g == 0), stop=False,
                                     skip_group_check=True)
                    mm = nc.tensor.matmul(o[:, P:T], val[:, 1, v], prob_t[:, g, T:T + P], start=False,
                                          stop=(g == NG - 1), skip_group_check=True)
                mm.then_inc(S.pv_done, 1)

            n = 5
            for hd in range(HEADS):
                scores(hd)
                gate_tile(n)
                n += 1
                if hd >= 1:
                    weigh(hd - 1)
                if hd < 3:
                    gate_tile(n)
                    n += 1
                flip(hd)
            pe.wait_ge(S.o_ready, 1)
            pe.wait_ge(S.scores_read, 2 * HEADS)
            weigh(HEADS - 1)
            for b in (0, 1, 2):
                if b == 0:
                    pe.wait_ge(S.pt_ready, HEADS)
                project(pe, l, 1, M_YB + b, 4 + b, hk)
            pe.wait_ge(S.att_ready, HEADS)
            project(pe, l, 1, M_YB + 3, 7, hk)
            pe.wait_ge(S.evac_done, 42)
            for j in range(2):
                p = M_YA + j
                slot_wait(pe, l, 1, p)
                for n in range(4):
                    for k in range(HEADS):
                        mm = nc.tensor.matmul(ps[:, 2 * j + n // 2, (n % 2) * T:(n % 2 + 1) * T],
                                              ring[:, p % RING, k * 512 + n * P:k * 512 + (n + 1) * P],
                                              att[:, k, :], start=(k == 0), stop=(k == HEADS - 1))
                mm.then_inc(S.tile_done, 1)
            pe.wait_ge(S.mem_ready, 1)
            for n in range(2):
                pe.wait_ge(S.yb_used, n + 1)
                project(pe, l, 1, M_KV0 + n, 4 + n, qk[:, 16:24, :])
            pe.wait_ge(S.merged, 2)
            for b in range(4):
                project(pe, l, 1, M_OUT + b, b, e_buf[1])
            for n in range(2, 8):
                if n < 4:
                    pe.wait_ge(S.yb_used, n + 1)
                else:
                    pe.wait_ge(S.evac_done, 42 + n - 3)
                (project if n < 4 else project_tok)(pe, l, 1, M_KV1 + n - 2, 4 + n % 4, qk[:, 16:24, :])
            pe.wait_ge(S.x_ready, 8)
            norm_pe(pe, 2, e_buf[0])
            pe.wait_ge(S.h_ready, 6)
            pe.wait_ge(S.rstd_ready, 3)
            for b in range(4):
                project(pe, l, 1, X_Q + b, b, h)

            def x_scores(hd):
                pe.wait_ge(S.evac_done, 50 + hd + 1)
                if hd < 2:
                    pe.wait_ge(S.evac_done, 50)
                else:
                    pe.wait_ge(S.scores_read, 2 * HEADS + hd - 1)
                for t in range(2):
                    for k in range(2):
                        mm = nc.tensor.matmul(ps[:, 4 + hd % 2, t * T:(t + 1) * T],
                                              qk[:, 8 + 2 * hd + k, t * P:(t + 1) * P], qk[:, 2 * hd + k, :],
                                              start=(k == 0), stop=(k == 1))
                mm.then_inc(S.scores_done, 1)

            def x_flip(hd):
                pe.wait_ge(S.probs_ready, HEADS + hd + 1)
                if hd >= 2:
                    pe.wait_ge(S.pt_ready, HEADS + hd - 1)
                for kt in range(2):
                    for t in range(2):
                        mm = nc.tensor.transpose(ps[:, 6 + hd % 2, kt * T + t * P:kt * T + (t + 1) * P],
                                                 prob[hd % 2][:, t * T + kt * P:t * T + (kt + 1) * P], ident)
                mm.then_inc(S.pt_done, 1)

            def x_weigh(hd):
                pe.wait_ge(S.pt_ready, HEADS + hd + 1)
                pt = prob_t[:].rearrange("p a b -> p (a b)")
                for dt in range(2):
                    for kt in range(2):
                        c = hd * XHD + dt * P
                        mm = nc.tensor.matmul(ps[:, hd, dt * T:(dt + 1) * T], val[:, kt, c:c + P],
                                              pt[:, (hd % 2) * 512 + kt * T:(hd % 2) * 512 + (kt + 1) * T],
                                              start=(kt == 0), stop=(kt == 1))
                mm.then_inc(S.pv_done, 1)

            x_scores(0)
            x_scores(1)
            for hd in range(HEADS):
                x_flip(hd)
                if hd + 2 < HEADS:
                    x_scores(hd + 2)
                x_weigh(hd)
            pe.wait_ge(S.att_ready, 2 * HEADS)
            for b in range(4):
                project(pe, l, 1, X_O + b, 4 + b, e_buf[1])
            pe.wait_ge(S.x_ready, 12)
            norm_pe(pe, 3, e_buf[0])
            ffn_pe(pe, FFN_B, 1, 3)

        def one_act(act, l):
            chain = Chain(act, S.act_chain)
            act.sem_inc(S.silu_done, 2)
            norm_act(act, chain, 0, 0, e_buf[0], between=lambda: first_high(act, l, 1, FFN_A, (0,)))
            first_high(act, l, 1, FFN_A, range(1, SPLITS))
            ffn_act(act, l, 1, FFN_A, 0)
            norm_act(act, chain, 1, 4, e_buf[0])

            def evac(p, out, bank, func=ACT.Copy, scale=1.0):
                act.wait_ge(S.tile_done, p + 1)
                src = ps[:, bank, :]
                if len(out.shape) == 3:
                    src = src.rearrange("p (a t) -> p a t", a=2)
                nc.scalar.activation(out, src, func, scale=scale).then_inc(S.evac_done, 1)

            for n in range(4):
                evac(M_F + n, hk[:, 2 * n:2 * n + 2, :], n % 3, ACT.Exp, -1.0)
            for n in range(4):
                evac(M_Q + n, hq[:, 2 * n:2 * n + 2, :], (4 + n) % 3, ACT.Copy, P ** -0.5)
            for n in range(4):
                evac(M_I + n, hi[:, :, n * T:(n + 1) * T], (8 + n) % 3)
            act.wait_ge(S.forget_ready, 1)
            nc.scalar.activation(hb[:], hb[:], ACT.Ln).then_inc(S.log_ready, 1)

            def decay(i):
                act.wait_ge(S.decay_arg, i + 1)
                nc.scalar.activation(e_buf[i % 2][:], e_buf[i % 2][:], ACT.Exp).then_inc(S.decay_exp, 1)

            for i in range(LEVELS + 1):
                for n in (2 * i, 2 * i + 1):
                    dst = qk[:, 2 * n:2 * n + 2, :] if n < 12 else val[:, :, (n - 12) * T:(n - 11) * T]
                    evac(M_QK + n, dst, (12 + n) % 3)
                if i < LEVELS:
                    decay(i)

            def gate(n):
                if n < 4:
                    if n == 0:
                        act.wait_ge(S.e_ready, LEVELS)
                    evac(M_OG + n, hb[:, 2 * n:2 * n + 2, :], n % 2, ACT.Silu)
                else:
                    buf = e_buf[0] if n >= 8 else e_buf[1]
                    if n == 4:
                        act.wait_ge(S.level_done, 2 * LEVELS)
                    evac(M_OG + n, buf[:, 2 * (n % 4):2 * (n % 4) + 2, :], n % 2, ACT.Tanh, 0.5)

            gate(0)
            gate(1)
            for g in range(2):
                act.wait_ge(S.o_done, g + 1)
                act.wait_ge(S.level_done, 2 * LEVELS + 2)
                part = ps[:, 4 + 2 * g:6 + 2 * g, :].rearrange("p b (a t) -> p (b a) t", a=2)
                nc.scalar.activation(hk[:, 4 * g:4 * g + 4, :], part, ACT.Copy)
                nc.scalar.activation(hq[:, 4 * g:4 * g + 4, :], part, ACT.Square).then_inc(S.o_copied, 1)
            gate(2)
            gate(3)
            act.wait_ge(S.o_var, 1)
            chain(nc.scalar.activation(hi_flat, hq_flat, ACT.Ln))
            nc.scalar.activation(hi_flat, hi_flat, ACT.Exp, scale=-0.5).then_inc(S.o_rstd, 1)
            gate(4)

            def exps(hd):
                act.wait_ge(S.max_ready, hd + 1)
                p = prob[hd % 2]
                nc.scalar.activation(p[:, 0:3 * P], p[:, 0:3 * P], ACT.Exp, bias=small[:, 0:1],
                                     accum_out=small[:, 2:3])
                nc.scalar.activation(p[:, 3 * P:], p[:, 3 * P:], ACT.Exp, bias=small[:, 1:2],
                                     accum_out=small[:, 3:4]).then_inc(S.exp_ready, 1)

            def flipped(hd):
                act.wait_ge(S.pt_done, hd + 1)
                if hd >= 1:
                    act.wait_ge(S.pv_done, hd)
                nc.scalar.activation(prob_t[:], ps[:, 2:5, 0:3 * P], ACT.Copy).then_inc(S.pt_ready, 1)

            def weighed(hd):
                act.wait_ge(S.pv_done, hd + 1)
                nc.scalar.activation(att[:, hd, :], ps[:, 7, (hd % 2) * T:(hd % 2 + 1) * T],
                                     ACT.Copy).then_inc(S.att_ready, 1)

            n = 5
            for hd in range(HEADS):
                exps(hd)
                gate(n)
                n += 1
                if hd >= 1:
                    weighed(hd - 1)
                if hd < 3:
                    gate(n)
                    n += 1
                flipped(hd)
            weighed(HEADS - 1)
            for n in range(8):
                p = M_KV0 + n if n < 2 else M_KV1 + n - 2
                dst = qk[:, 2 * n:2 * n + 2, :] if n < 4 else val[:, :, (n - 4) * T:(n - 3) * T]
                evac(p, dst, 4 + n % 4)
            norm_act(act, chain, 2, 8, e_buf[0])
            for n in range(4):
                evac(X_Q + n, qk[:, 8 + 2 * n:10 + 2 * n, :], n)

            def x_exps(hd):
                act.wait_ge(S.max_ready, HEADS + hd + 1)
                p = prob[hd % 2]
                for t in range(2):
                    ins = nc.scalar.activation(p[:, t * T:(t + 1) * T], p[:, t * T:(t + 1) * T], ACT.Exp,
                                               bias=small[:, 4 * (hd % 2) + t:4 * (hd % 2) + t + 1],
                                               accum_out=small[:, 4 * (hd % 2) + 2 + t:4 * (hd % 2) + 3 + t])
                ins.then_inc(S.exp_ready, 1)

            def x_flipped(hd):
                act.wait_ge(S.pt_done, HEADS + hd + 1)
                if hd >= 2:
                    act.wait_ge(S.pv_done, HEADS + hd - 1)
                pt = prob_t[:].rearrange("p a b -> p (a b)")
                nc.scalar.activation(pt[:, (hd % 2) * 512:(hd % 2 + 1) * 512], ps[:, 6 + hd % 2, :],
                                     ACT.Copy).then_inc(S.pt_ready, 1)

            def x_weighed(hd):
                act.wait_ge(S.pv_done, HEADS + hd + 1)
                nc.scalar.activation(e_buf[1][:, 2 * hd:2 * hd + 2, :],
                                     ps[:, hd, :].rearrange("p (a t) -> p a t", a=2),
                                     ACT.Copy).then_inc(S.att_ready, 1)

            x_exps(0)
            for hd in range(HEADS):
                if hd + 1 < HEADS:
                    x_exps(hd + 1)
                x_flipped(hd)
                x_weighed(hd)
            first_high(act, l, 1, FFN_B)
            norm_act(act, chain, 3, 12, e_buf[0])
            ffn_act(act, l, 1, FFN_B, 1)

        def one_dve(dve, l):
            chain = Chain(dve, S.dve_chain)
            dve.sem_inc(S.prod_done, 2)
            chain(nc.vector.tensor_copy(v_now[:, 0:V1_W], vec_sb[:, bass.ds(l * V1_W + VEC_1, V1_W)]))
            chain(nc.vector.tensor_copy(lb_now[:, 1, :], lb[:].rearrange("p l k -> p (l k)")[:, bass.ds(l * KD, KD)]))
            nc.vector.tensor_scalar(lb_now[:, 0, :], lb_now[:, 1, :], -1.0, 1.0, ALU.mult, ALU.add)
            nc.vector.memset(small[:, 15:16], 0.0).then_inc(S.vec_ready, 1)
            norm_dve(dve, chain, 0, 0, v_now[:, V1_FFN1:V1_FFN1 + KD], split=True,
                     between=lambda: first_low(dve, FFN_A, 0, (0,)))
            ffn_dve(dve, FFN_A, 0, 1)
            residual(dve, lambda b: FFN_A + FFN_TILES - 1, 4, 0.5)
            norm_dve(dve, chain, 1, 4, v_now[:, V1_MIX:V1_MIX + KD])

            dve.wait_ge(S.evac_done, 4)
            chain(nc.vector.tensor_scalar(hk[:], hk[:], 1.0, None, ALU.add))
            chain(nc.vector.reciprocal(hk[:], hk[:]))
            for hd in range(HG):
                ins = nc.vector.tensor_scalar(hk[:, hd, :], hk[:, hd, :], lb_now[:, 0, hd:hd + 1],
                                              lb_now[:, 1, hd:hd + 1], ALU.mult, ALU.add)
            chain(ins)
            nc.vector.tensor_scalar(hb[:], hk[:], 2.0 ** -64, None, ALU.max).then_inc(S.forget_ready, 1)
            chain(nc.vector.tensor_scalar(hk[:], hk[:], -1.0, 1.0, ALU.mult, ALU.add))
            keep = e_buf[1][:].rearrange("p k t -> p (k t)")
            chain(nc.vector.memset(keep, 1.0))
            chain(nc.vector.memset(keep.rearrange("p (g c) -> p g c", c=RUN)[:, :, 0:1], 0.0))
            dve.wait_ge(S.log_ready, 1)
            nc.vector.tensor_tensor_scan(b_flat, keep, b_flat, 0.0, ALU.mult, ALU.add).then_inc(S.cumsum_ready, 1)
            dve.wait_ge(S.cumsum_ready, 1)

            def args(i):
                half = levels[i]
                if i >= 2:
                    dve.wait_ge(S.level_done, 2 * (i - 1))
                elif i == 0:
                    dve.wait_ge(S.h_ready, 4)
                lo, hi_ = halves(e_buf[i % 2], half)
                b_lo, b_hi = halves(hb, half)
                if half == 2 * RUN:
                    e = e_buf[i % 2][:].rearrange("p k (c n) -> p k c n", n=RUN)
                    b = hb[:].rearrange("p k (c n) -> p k c n", n=RUN)
                    end = [b[:, :, c, RUN - 1:RUN].broadcast_to([P, KD, RUN]) for c in range(3)]
                    nc.vector.tensor_tensor(e[:, :, 1, :], end[1], b[:, :, 1, :], ALU.subtract)
                    nc.vector.tensor_copy(e[:, :, 2, :], b[:, :, 2, :])
                    nc.vector.tensor_tensor(e[:, :, 3, :], b[:, :, 3, :], end[2], ALU.add)
                    chain(nc.vector.tensor_tensor(e[:, :, 0, :], end[0], b[:, :, 0, :], ALU.subtract))
                    nc.vector.tensor_tensor(e[:, :, 0, :], e[:, :, 0, :], end[1], ALU.add).then_inc(S.decay_arg, 1)
                    return
                mid = b_lo[:, :, half - 1:half].broadcast_to([P, KD * T // (2 * half), half])
                nc.vector.tensor_tensor(lo, mid, b_lo, ALU.subtract)
                if half == RUN:
                    nc.vector.tensor_copy(hi_, b_hi).then_inc(S.decay_arg, 1)
                else:
                    nc.vector.tensor_tensor(hi_, b_hi, mid, ALU.subtract).then_inc(S.decay_arg, 1)

            def factors(i):
                if i == 0:
                    dve.wait_ge(S.evac_done, 8)
                half = levels[i]
                dve.wait_ge(S.decay_exp, i + 1)
                lo, hi_ = halves(e_buf[i % 2], half)
                nc.vector.tensor_tensor(lo, lo, halves(hk, half)[0], ALU.mult)
                nc.vector.tensor_tensor(hi_, hi_, halves(hq, half)[1], ALU.mult).then_inc(S.e_ready, 1)

            def gather(i):
                if i == 0:
                    dve.wait_ge(S.a_zeroed, 1)
                for g in range(2):
                    dve.wait_ge(S.level_done, 2 * i + g + 1)
                    if i == 0:
                        ins = nc.vector.tensor_copy(a_hg[:, 4 * g:4 * g + 4, 1, :],
                                                    ps[:, 4 + 2 * g, :].rearrange("p (a t) -> p a t", a=4))
                    else:
                        src = ps[:, 4 + 2 * g:6 + 2 * g, :].rearrange("p b (a two t) -> p (b a) two t", a=2, two=2)
                        for t in range(2):
                            ins = nc.vector.copy_predicated(
                                a_hg[:, 4 * g:4 * g + 4, 2 * t, :],
                                lm[:, i - 1, :].unsqueeze(1).broadcast_to([P, 4, P]), src[:, :, t, :])
                    ins.then_inc(S.level_used, 1)

            def rot_scale(n):
                dve.wait_ge(S.rot_done, n + 1)
                if n >= 1:
                    dve.wait_ge(S.rope_done, n)
                nc.vector.tensor_tensor(rope_b[:], ps[:, 3, :].rearrange("p (a t) -> p a t", a=2),
                                        sin1[:].unsqueeze(1).broadcast_to([P, 2, T]),
                                        ALU.mult).then_inc(S.rot_scaled, 1)

            args(0)
            for i in range(LEVELS + 1):
                if i + 1 < LEVELS:
                    args(i + 1)
                for n in (2 * i - 2, 2 * i - 1):
                    if 0 <= n < 12:
                        rot_scale(n)
                if i < LEVELS:
                    factors(i)
                if i >= 1:
                    gather(i - 1)
            gather(LEVELS)

            dve.wait_ge(S.o_ss, 1)
            nc.vector.tensor_scalar(hq_flat, ps[:, 4:8, :].rearrange("p b t -> p (b t)"), 1.0 / P, EPS,
                                    ALU.mult, ALU.add).then_inc(S.o_var, 1)
            dve.wait_ge(S.o_rstd, 1)
            refine(chain, hi_flat, hq_flat)
            hk_flat = hk[:].rearrange("p k t -> p (k t)")
            chain(nc.vector.tensor_tensor(hk_flat, hk_flat, hi_flat, ALU.mult))
            dve.wait_ge(S.evac_done, 34)
            for hd in range(HG):
                ins = nc.vector.scalar_tensor_tensor(out=hk[:, hd, :], in0=hk[:, hd, :],
                                                     scalar=v_now[:, V1_HEAD + hd:V1_HEAD + hd + 1],
                                                     in1=hb[:, hd, :], op0=ALU.mult, op1=ALU.mult)
            ins.then_inc(S.o_ready, 1)

            def soften(hd, parts, count, mask, scale, at):
                p = prob[hd % 2]
                dve.wait_ge(S.scores_done, count + 1)
                for src, lo, hi_ in parts:
                    if mask is None:
                        ins = nc.vector.tensor_scalar(p[:, lo:hi_], src, scale, None, ALU.mult)
                    else:
                        ins = nc.vector.scalar_tensor_tensor(out=p[:, lo:hi_], in0=src, scalar=scale,
                                                             in1=mask[:, lo:hi_], op0=ALU.mult, op1=ALU.add)
                    if mask is not None:
                        ins.then_inc(S.scores_read, 1)
                if mask is None:
                    ins.then_inc(S.scores_read, 1)
                    dve.wait_ge(S.scores_read, 2 * HEADS + hd + 1)
                    cuts = ((0, T), (T, 2 * T))
                else:
                    dve.wait_ge(S.scores_read, 2 * (hd + 1))
                    cuts = ((0, 3 * P), (3 * P, 9 * P))
                for t, (lo, hi_) in enumerate(cuts):
                    ins = nc.vector.tensor_reduce(small[:, at + t:at + t + 1], p[:, lo:hi_], AX.X, ALU.max,
                                                  negate=True)
                ins.then_inc(S.max_ready, 1)

            def normalise(hd, count, at, cuts):
                p = prob[hd % 2]
                dve.wait_ge(S.exp_ready, count + 1)
                chain(nc.vector.reciprocal(small[:, at + 2:at + 4], small[:, at + 2:at + 4]))
                for t, (lo, hi_) in enumerate(cuts):
                    ins = nc.vector.tensor_scalar(p[:, lo:hi_], p[:, lo:hi_], small[:, at + 2 + t:at + 3 + t],
                                                  None, ALU.mult)
                ins.then_inc(S.probs_ready, 1)

            for hd in range(HEADS):
                parts = ((ps[:, 4, 0:3 * P], 0, 3 * P),
                         (ps[:, 5:7, :].rearrange("p b t -> p (b t)")[:, 0:6 * P], 3 * P, 9 * P))
                if hd >= 2:
                    dve.wait_ge(S.pt_done, hd - 1)
                soften(hd, parts, hd, C(C_M1, 9 * P), DH ** -0.5, 0)
                normalise(hd, hd, 0, ((0, 3 * P), (3 * P, 9 * P)))

            dve.wait_ge(S.evac_done, 42)
            for b in range(4):
                dve.wait_ge(S.tile_done, M_YB + b + 1)
                part = e_buf[0][:, 2 * b:2 * b + 2, :].rearrange("p k t -> p (k t)")
                nc.vector.scalar_tensor_tensor(out=part, in0=part, scalar=1.0, in1=ps[:, 4 + b, :],
                                               op0=ALU.add, op1=ALU.mult).then_inc(S.yb_used, 1)
            dve.wait_ge(S.yb_used, 4)
            for j in range(2):
                dve.wait_ge(S.tile_done, M_YA + j + 1)
                part = e_buf[1][:, 4 * j:4 * j + 4, :].rearrange("p k t -> p (k t)")
                nc.vector.scalar_tensor_tensor(out=part, in0=part, scalar=1.0,
                                               in1=ps[:, 2 * j:2 * j + 2, :].rearrange("p b t -> p (b t)"),
                                               op0=ALU.add, op1=ALU.mult).then_inc(S.ya_used, 1)
                dve.wait_ge(S.ya_used, j + 1)
                nc.vector.tensor_tensor(part, part, e_buf[0][:, 4 * j:4 * j + 4, :].rearrange("p k t -> p (k t)"),
                                        ALU.add).then_inc(S.merged, 1)
            residual(dve, lambda b: M_OUT + b, 0, 0.5)
            norm_dve(dve, chain, 2, 8, v_now[:, V1_X:V1_X + KD])
            x_cuts = ((0, T), (T, 2 * T))

            def x_soften(hd):
                if hd >= 2:
                    dve.wait_ge(S.pt_done, HEADS + hd - 1)
                soften(hd, ((ps[:, 4 + hd % 2, :], 0, 2 * T),), HEADS + hd, None, XHD ** -0.5, 4 * (hd % 2))

            x_soften(0)
            for hd in range(HEADS):
                if hd == 0:
                    x_soften(1)
                normalise(hd, HEADS + hd, 4 * (hd % 2), x_cuts)
                if 1 <= hd < HEADS - 1:
                    x_soften(hd + 1)
            first_low(dve, FFN_B, 1, range(SPLITS))
            residual(dve, lambda b: X_O + b, 4, 1.0)
            norm_dve(dve, chain, 3, 12, v_now[:, V1_FFN2:V1_FFN2 + KD], split=True)
            ffn_dve(dve, FFN_B, 1, SPLITS)
            residual(dve, lambda b: FFN_B + FFN_TILES - 1, 4, 0.5)

        def one_pool(pool, l):
            pool.wait_ge(S.x_ready, 4)
            nc.gpsimd.memset(a_hg[:], 0.0).then_inc(S.a_zeroed, 1)
            for n in range(12):
                part = qk[:, 2 * n:2 * n + 2, :]
                pool.wait_ge(S.evac_done, 12 + n + 1)
                if n >= 1:
                    pool.wait_ge(S.rope_done, n)
                nc.gpsimd.tensor_tensor(rope_a[:], part, cos1[:].unsqueeze(1).broadcast_to([P, 2, T]),
                                        ALU.mult).then_inc(S.pool_chain, 1)
                pool.wait_ge(S.pool_chain, n + 1)
                pool.wait_ge(S.rot_scaled, n + 1)
                nc.gpsimd.tensor_tensor(part, rope_a[:], rope_b[:], ALU.add).then_inc(S.rope_done, 1)
            pool.wait_ge(S.scores_done, HEADS)
            pool.wait_ge(S.vec_ready, 1)
            for k in range(KD):
                ins = nc.gpsimd.tensor_scalar(qk[:, 16 + k, :], mem[:, k, :], v_now[:, V1_MEM + k:V1_MEM + k + 1],
                                              1.0, ALU.mult, ALU.mult)
            ins.then_inc(S.mem_ready, 1)

        with nc.Fori(0, DEPTH) as l:
            with nc.Block() as block:
                @block.sync
                def _(sp):
                    stream_in(sp, l, TILES_1, 0, False)

                @block.tensor
                def _(pe):
                    one_pe(pe, l)

                @block.scalar
                def _(act):
                    one_act(act, l)

                @block.vector
                def _(dve):
                    one_dve(dve, l)

                @block.gpsimd
                def _(pool):
                    one_pool(pool, l)
            nc.all_engine_barrier(sems_to_clear=layer_sems)

        with nc.Block() as block:
            @block.sync
            def _(sp):
                sp.dma_start(con_sb[:, C_OWN:C_W], con[:, C_OWN + C_NEXT:C_W + C_NEXT]).then_inc(S.load, 16)
                sp.wait_ge(S.load, 16)

            @block.tensor
            def _(pe):
                norm_pe(pe, 0, e_buf[0])

            @block.scalar
            def _(act):
                nc.scalar.activation(silu_c[:], vec_sb[:, VEC_C:VEC_C + KD], ACT.Silu)
                norm_act(act, Chain(act, S.act_chain), 0, 0, e_buf[0])

            @block.vector
            def _(dve):
                rstd_dve(dve, Chain(dve, S.dve_chain), 0)
                for k in range(KD):
                    nc.vector.scalar_tensor_tensor(out=x[:, k, :], in0=x[:, k, :],
                                                   scalar=vec_sb[:, VEC_FIN + k:VEC_FIN + k + 1], in1=rstd[:],
                                                   op0=ALU.mult, op1=ALU.mult)
        nc.all_engine_barrier(sems_to_clear=layer_sems)

        fq = qk
        ropes = ((0, 2), (2, 2), (4, 1), (5, 2), (7, 2), (9, 2), (11, 2))
        N_ROPE = len(ropes)
        NORMED = 3
        w_idx = small2
        score = hb[:].rearrange("p k t -> p (k t)")[:, 0:3 * P]
        dsa_mask = hb[:].rearrange("p k t -> p (k t)")[:, 3 * P:6 * P]
        m8 = hb[:].rearrange("p k t -> p (k t)")[:, 6 * P:6 * P + 16]
        relu = e_buf[0][:].rearrange("p k t -> p (k t)").rearrange("p (u n) -> p u n", u=4)
        st = a_hg[:].rearrange("p a b c -> p (a b c)").rearrange("p (u n) -> p u n", u=8)
        pt2 = prob_t
        units = [(0, (0, 2, 4, 6)), (0, (1, 3, 5, 7))] + [(1, hs) for hs in ((0, 2), (1, 3), (4, 6), (5, 7))]
        HEADS_2 = HA + HB
        LATE_AT = 3 * P

        def unit_cols(qt, i):
            n = P * (qt + 1)
            return slice(i * n, (i + 1) * n)

        def modulation(pe, l, p0, tiles, bank, at):
            for j in tiles:
                slot_wait(pe, l, 2, p0 + j)
                for n in range(2):
                    c = at + 2 * j + n
                    for k in range(KD):
                        mm = nc.tensor.matmul(ps[:, bank, c:c + 1], block_w(p0 + j, k, n), silu_c[:, k:k + 1],
                                              start=(k == 0), stop=(k == KD - 1))
                mm.then_inc(S.tile_done, 1)

        def two_pe(pe, l):
            norm_pe(pe, 0, e_buf[0])
            modulation(pe, l, ADA, range(N_FRONT), 3, 0)
            ffn_pe(pe, FFN_C, 0, 0)
            modulation(pe, l, ADA_MID, range(KD // 2), 1, 0)
            modulation(pe, l, ADA_MID, range(KD // 2, N_MID), 3, 0)
            pe.wait_ge(S.x_ready, 4)
            norm_pe(pe, 1, e_buf[0])
            pe.wait_ge(S.h_ready, 4)

            def tile(n):
                p = Z_QI + n
                if n >= 3:
                    pe.wait_ge(S.evac_done, n - 2)
                if n == 2:
                    slot_wait(pe, l, 2, p)
                    for k in range(KD):
                        nc.tensor.matmul(ps[0:HD, 2, 0:T], ring[:, p % RING, k * T:k * T + HD], h[:, k, :],
                                         start=(k == 0), stop=(k == KD - 1))
                    for t in range(2):
                        for k in range(KD):
                            mm = nc.tensor.matmul(ps[:, 2, T + t * IDX:T + (t + 1) * IDX],
                                                  h[:, k, t * P:(t + 1) * P],
                                                  ring[:, p % RING, k * T + HD:k * T + HD + IDX],
                                                  start=(k == 0), stop=(k == KD - 1))
                    mm.then_inc(S.tile_done, 1)
                elif 7 <= n < 11:
                    project_tok(pe, l, 2, p, n % 3, h)
                else:
                    project(pe, l, 2, p, n % 3, h)

            def head_sums(j):
                pe.wait_ge(S.head_sq, j - NORMED + 1)
                pe.wait_ge(S.rot_scaled, j)
                nc.tensor.matmul(ps[:, 3, :], C(C_BD, P),
                                 e_buf[1][:, 2 * (j - NORMED):2 * (j - NORMED) + 2, :].rearrange("p k t -> p (k t)"),
                                 start=True, stop=True).then_inc(S.head_ss, 1)

            def rotate(j):
                at, n = ropes[j]
                if j >= NORMED:
                    pe.wait_ge(S.head_ready, j - NORMED + 1)
                else:
                    pe.wait_ge(S.evac_done, j + 1)
                    if j >= 1:
                        pe.wait_ge(S.rot_scaled, j)
                r = HD if n == 1 else P
                nc.tensor.matmul(ps[0:r, 3, 0:n * T], con_sb[0:r, C_R2:C_R2 + r],
                                 fq[0:r, at:at + n, :].rearrange("p k t -> p (k t)"),
                                 start=True, stop=True).then_inc(S.rot_done, 1)

            tile(0)
            tile(1)
            rotate(0)
            tile(2)
            rotate(1)
            tile(3)
            rotate(2)
            for j in range(NORMED, N_ROPE):
                head_sums(j)
                tile(j + 1)
                rotate(j)
            for u, (qt, heads) in enumerate(units):
                pe.wait_ge(S.ki_ready, 1)
                if u >= 4:
                    pe.wait_ge(S.relu_ready, u - 3)
                for i, j in enumerate(heads):
                    r = slice(HD * (j % 2), HD * (j % 2 + 1))
                    mm = nc.tensor.matmul(ps[:, 4 + u % 4, unit_cols(qt, i)], fq[r, j // 2, qt * P:(qt + 1) * P],
                                          fq[r, 4, 0:P * (qt + 1)], start=True, stop=True)
                mm.then_inc(S.logit_done, 1)
            for n in range(8, 15):
                tile(n)

            def scores(n):
                if n < 2:
                    pe.wait_ge(S.relu_ready, len(units))
                    pe.wait_ge(S.rope_done, N_ROPE)
                else:
                    pe.wait_ge(S.scores_read, n - 1)
                q, k = (9, 11) if n < HA else (5, 7)
                r, i = slice(HD * (n % 2), HD * (n % 2 + 1)), (n % HA) // 2
                nc.tensor.matmul(ps[:, 4 + n % 2, 0:P], fq[r, q + i, 0:P], fq[r, k + i, 0:P], start=True, stop=True)
                nc.tensor.matmul(ps[:, 4 + n % 2, P:3 * P], fq[r, q + i, P:T], fq[r, k + i, :], start=True,
                                 stop=True).then_inc(S.scores_done, 1)

            def sticks(c):
                pe.wait_ge(S.evac_done, 15)
                if c >= 2:
                    pe.wait_ge(S.zm_ready, c - 1)
                r = slice(HD * (c % 2), HD * (c % 2 + 1))
                q, k = fq[r, 13 + c // 2, :], fq[r, 17 + c // 2, :]
                nc.tensor.matmul(ps[:, c % 2, 0:T], k[:, 0:P], q, start=True, stop=True)
                nc.tensor.matmul(ps[:, c % 2, T:3 * P], k[:, P:T], q[:, P:T], start=True,
                                 stop=True).then_inc(S.z_done, 1)

            def flip(n):
                pe.wait_ge(S.probs_ready, n + 1)
                if n >= 1:
                    pe.wait_ge(S.pt_ready, n)
                for c, at in enumerate((0, P, 2 * P)):
                    mm = nc.tensor.transpose(ps[:, 6, c * P:(c + 1) * P], prob[n % 2][:, at:at + P], ident)
                mm.then_inc(S.pt_done, 1)

            def sums(c):
                pe.wait_ge(S.l_ready, c + 1)
                if c >= 1:
                    pe.wait_ge(S.arg_ready, c)
                ll = st[:, 4 + c % 2, :]
                nc.tensor.matmul(ps[:, 2, 0:T], C(C_TRI, P), ll[:, 0:T], start=True, stop=False,
                                 skip_group_check=True)
                nc.tensor.matmul(ps[:, 2, P:T], ones, ll[:, T:3 * P], start=False, stop=True,
                                 skip_group_check=True)
                nc.tensor.matmul(ps[:, 2, T:3 * P], C(C_TRI, P), ll[:, T:3 * P], start=True, stop=True,
                                 skip_group_check=True).then_inc(S.cum_done, 1)

            def weigh(n, w, v, bank, ready, used, done):
                pe.wait_ge(ready, n + 1)
                if n >= 2:
                    pe.wait_ge(used, n // 2)
                r = slice(HD * (n % 2), HD * (n % 2 + 1))
                nc.tensor.matmul(ps[r, bank, 0:T], val[:, 0, v:v + HD], w[:, 0:T], start=True, stop=False,
                                 skip_group_check=True)
                nc.tensor.matmul(ps[r, bank, P:T], val[:, 1, v:v + HD], w[:, T:3 * P], start=False, stop=True,
                                 skip_group_check=True).then_inc(done, 1)

            for n in range(HEADS_2 + 1):
                if n < HEADS_2:
                    scores(n)
                    sticks(n)
                if n == 0:
                    modulation(pe, l, Z_LATE, range(N_LATE // 2), 2, LATE_AT)
                if n >= 1:
                    i = n - 1
                    flip(i)
                    sums(i)
                    weigh(i, pt2[:, i % 2, :], i * HD, 7, S.pt_ready, S.att_ready, S.pv_done)
                    weigh(i, st[:, 6 + i % 2, :], (HEADS_2 + i) * HD, 3, S.a_ready, S.o_copied, S.o_done)
            for b in range(4):
                pe.wait_ge(S.sq_ready, 5)
                if b == 0:
                    pe.wait_ge(S.scores_read, HEADS_2)
                    pe.wait_ge(S.pt_ready, HEADS_2)
                mm = nc.tensor.matmul(ps[:, 4 + b, :], C(C_BD, P),
                                      e_buf[0][:, 2 * b:2 * b + 2, :].rearrange("p k t -> p (k t)"),
                                      start=True, stop=True)
            mm.then_inc(S.o_ss, 1)
            pe.wait_ge(S.arg_ready, HEADS_2)
            modulation(pe, l, Z_LATE, range(N_LATE // 2, N_LATE), 2, LATE_AT)
            pe.wait_ge(S.o_ready, 1)
            for b in range(4):
                if b == 2:
                    pe.wait_ge(S.mod_ready, 1)
                project(pe, l, 2, Z_O + b, b, hk)
            pe.wait_ge(S.x_ready, 8)
            norm_pe2(pe)
            ffn_pe(pe, FFN_D, 1, 2)

        def norm_pe2(pe):
            for k in range(KD):
                if k % 4 == 0:
                    pe.wait_ge(S.sq_ready, 5 + k // 4 + 1)
                mm = nc.tensor.matmul(ps[:, 0, 0:T], ones, e_buf[0][:, k, :], start=(k == 0), stop=(k == KD - 1))
            mm.then_inc(S.ss_ready, 1)

        def two_act(act, l):
            chain = Chain(act, S.act_chain)
            act.sem_inc(S.silu_done, 2)
            norm_act(act, chain, 0, 0, e_buf[0])
            first_high(act, l, 2, FFN_C)
            ffn_act(act, l, 2, FFN_C, 0)
            norm_act(act, chain, 1, 4, e_buf[0])

            def evac(n):
                p = Z_QI + n
                act.wait_ge(S.tile_done, p + 1)
                src = ps[:, n % 3, :].rearrange("p (a t) -> p a t", a=2)
                if n == 2:
                    nc.scalar.activation(fq[0:HD, 4, :], ps[0:HD, 2, 0:T], ACT.Copy)
                    nc.scalar.activation(w_idx[:], ps[:, 2, T:T + 2 * IDX], ACT.Copy).then_inc(S.evac_done, 1)
                elif n < 2:
                    nc.scalar.activation(fq[:, 2 * n:2 * n + 2, :], src, ACT.Copy).then_inc(S.evac_done, 1)
                elif n < 7:
                    at = 5 + 2 * (n - 3)
                    if n == 3:
                        act.wait_ge(S.h_ready, 4)
                    nc.scalar.activation(e_buf[1][:, 2 * (n - 3):2 * (n - 3) + 2, :], src,
                                         ACT.Square).then_inc(S.head_sq, 1)
                    nc.scalar.activation(fq[:, at:at + 2, :], src, ACT.Copy).then_inc(S.evac_done, 1)
                elif n < 11:
                    nc.scalar.activation(val[:, :, (n - 7) * T:(n - 6) * T], src, ACT.Copy).then_inc(S.evac_done, 1)
                else:
                    at = 13 + 2 * (n - 11)
                    nc.scalar.activation(fq[:, at:at + 2, :], src, ACT.Copy).then_inc(S.evac_done, 1)

            def head_rstd(j):
                i = j - NORMED
                act.wait_ge(S.head_var, i + 1)
                part = e_buf[1][:, 2 * i:2 * i + 2, :]
                chain(nc.scalar.activation(part, e_buf[0][:, 2 * i:2 * i + 2, :], ACT.Ln))
                nc.scalar.activation(part, part, ACT.Exp, scale=-0.5).then_inc(S.head_rs, 1)

            for n in range(4):
                evac(n)
            act.wait_ge(S.rope_done, 3)
            nc.scalar.activation(fq[HD:P, 4, :], fq[0:HD, 4, :], ACT.Copy).then_inc(S.ki_ready, 1)
            for j in range(NORMED, N_ROPE):
                head_rstd(j)
                evac(j + 1)
            act.wait_ge(S.head_ready, N_ROPE - NORMED)
            for u in range(len(units)):
                act.wait_ge(S.logit_done, u + 1)
                if u >= 4:
                    act.wait_ge(S.relu_used, u - 3)
                nc.scalar.activation(relu[:, u % 4, :], ps[:, 4 + u % 4, :], ACT.Relu).then_inc(S.relu_ready, 1)
            for n in range(8, 15):
                evac(n)

            def exps(n):
                act.wait_ge(S.max_ready, n + 1)
                p, at = prob[n % 2], 4 * (n % 2)
                nc.scalar.activation(p[:, 0:P], p[:, 0:P], ACT.Exp, bias=small[:, at:at + 1],
                                     accum_out=small[:, at + 2:at + 3])
                nc.scalar.activation(p[:, P:3 * P], p[:, P:3 * P], ACT.Exp, bias=small[:, at + 1:at + 2],
                                     accum_out=small[:, at + 3:at + 4]).then_inc(S.exp_ready, 1)

            def softplus(c):
                act.wait_ge(S.zm_ready, c + 1)
                if c >= 2:
                    act.wait_ge(S.l_ready, c - 1)
                zm, sp_ = st[:, c % 2, :], st[:, 2 + c % 2, :]
                chain(nc.scalar.activation(sp_, zm, ACT.Abs))
                chain(nc.scalar.activation(sp_, sp_, ACT.Exp, scale=-1.0))
                nc.scalar.activation(sp_, sp_, ACT.Ln, bias=one[:]).then_inc(S.soft_ready, 1)

            def after(i):
                act.wait_ge(S.pt_done, i + 1)
                if i >= 2:
                    act.wait_ge(S.pv_done, i - 1)
                nc.scalar.activation(pt2[:, i % 2, :], ps[:, 6, 0:3 * P], ACT.Copy).then_inc(S.pt_ready, 1)
                act.wait_ge(S.arg_ready, i + 1)
                nc.scalar.activation(st[:, 6 + i % 2, :], st[:, 6 + i % 2, :], ACT.Exp).then_inc(S.a_ready, 1)
                if i % 2:
                    act.wait_ge(S.pv_done, i + 1)
                    nc.scalar.activation(hk[:, i // 2, :], ps[:, 7, 0:T], ACT.Copy).then_inc(S.att_ready, 1)
                    act.wait_ge(S.o_done, i + 1)
                    nc.scalar.activation(hk[:, 4 + i // 2, :], ps[:, 3, 0:T], ACT.Copy).then_inc(S.o_copied, 1)

            for n in range(HEADS_2 + 1):
                if n < HEADS_2:
                    exps(n)
                    softplus(n)
                if n >= 1:
                    after(n - 1)
            act.wait_ge(S.o_copied, HEADS_2 // 2)
            act.wait_ge(S.att_ready, HEADS_2 // 2)
            nc.scalar.activation(e_buf[0][:], hk[:], ACT.Square).then_inc(S.sq_ready, 1)
            act.wait_ge(S.o_var, 1)
            chain(nc.scalar.activation(e_buf[1][:], e_buf[0][:], ACT.Ln))
            nc.scalar.activation(e_buf[1][:], e_buf[1][:], ACT.Exp, scale=-0.5).then_inc(S.o_rstd, 1)
            first_high(act, l, 2, FFN_D, (0,))
            norm_act(act, chain, 2, 8, e_buf[0])
            first_high(act, l, 2, FFN_D, range(1, SPLITS))
            ffn_act(act, l, 2, FFN_D, 1)

        def two_dve(dve, l):
            chain = Chain(dve, S.dve_chain)
            dve.sem_inc(S.prod_done, 2)
            chain(nc.vector.tensor_copy(v_now[:], vec_sb[:, bass.ds(l * V2_W + VEC_2, V2_W)]))
            rstd_dve(dve, chain, 0)
            first_low(dve, FFN_C, 0, (0,))
            parts = [mod[:, i * KD:(i + 1) * KD] for i in range(9)]

            def add_bias(group, end, src):
                to = slice(group * KD, end * KD)
                chain(nc.vector.tensor_tensor(mod[:, to], src, v_now[:, V2_ADA + to.start:V2_ADA + to.stop], ALU.add))

            def gain(i):
                chain(nc.vector.scalar_tensor_tensor(out=parts[3 * i + 1], in0=parts[3 * i + 1], scalar=1.0,
                                                     in1=v_now[:, V2_NORM + i * KD:V2_NORM + (i + 1) * KD],
                                                     op0=ALU.add, op1=ALU.mult))

            dve.wait_ge(S.tile_done, ADA + N_FRONT)
            add_bias(0, 2, ps[:, 3, 0:2 * KD])
            gain(0)
            norm_dve(dve, chain, 0, 0, parts[1], parts[0], split=True, stats=False)
            ffn_dve(dve, FFN_C, 0, 1)
            dve.wait_ge(S.tile_done, ADA_MID + KD // 2)
            add_bias(2, 3, ps[:, 1, 0:KD])
            chain(nc.vector.tensor_scalar(parts[2], parts[2], 0.5, None, ALU.mult))
            residual(dve, lambda b: FFN_C + FFN_TILES - 1, 4, parts[2])
            dve.wait_ge(S.tile_done, ADA_MID + N_MID)
            add_bias(3, 5, ps[:, 3, KD:3 * KD])
            gain(1)
            norm_dve(dve, chain, 1, 4, parts[4], parts[3])

            def rope(j):
                at, n = ropes[j]
                r = HD if n == 1 else P
                if j >= NORMED:
                    i = j - NORMED
                    vv, rr = (e[:, 2 * i:2 * i + 2, :].rearrange("p k t -> p (k t)") for e in e_buf)
                    dve.wait_ge(S.head_ss, i + 1)
                    nc.vector.tensor_scalar(vv, ps[:, 3, :], 1.0 / HD, EPS, ALU.mult, ALU.add).then_inc(S.head_var, 1)
                    dve.wait_ge(S.head_rs, i + 1)
                    refine(chain, rr, vv)
                    dve.wait_ge(S.evac_done, j + 1)
                    part = fq[:, at:at + 2, :].rearrange("p k t -> p (k t)")
                    g = V2_QK + (2, 3, 0, 1)[i]
                    nc.vector.scalar_tensor_tensor(out=part, in0=part, scalar=v_now[:, g:g + 1],
                                                   in1=e_buf[1][:, 2 * i:2 * i + 2, :].rearrange("p k t -> p (k t)"),
                                                   op0=ALU.mult, op1=ALU.mult).then_inc(S.head_ready, 1)
                dve.wait_ge(S.rot_done, j + 1)
                if j >= 1:
                    dve.wait_ge(S.rope_done, j)
                nc.vector.tensor_tensor(rope_b[0:r, 0:n, :], ps[0:r, 3, 0:n * T].rearrange("p (a t) -> p a t", a=n),
                                        con_sb[0:r, C_SIN:C_SIN + T].unsqueeze(1).broadcast_to([r, n, T]),
                                        ALU.mult).then_inc(S.rot_scaled, 1)

            for j in range(N_ROPE):
                rope(j)
            dve.wait_ge(S.evac_done, 3)
            for u, (qt, heads) in enumerate(units):
                dve.wait_ge(S.relu_ready, u + 1)
                part = score[:, 0:P] if qt == 0 else score[:, P:3 * P]
                for i, j in enumerate(heads):
                    w = w_idx[:, qt * IDX + j:qt * IDX + j + 1]
                    src = relu[:, u % 4, unit_cols(qt, i)]
                    if j == 0:
                        ins = nc.vector.tensor_scalar(part, src, w, None, ALU.mult)
                    else:
                        ins = nc.vector.scalar_tensor_tensor(out=part, in0=src, scalar=w, in1=part,
                                                             op0=ALU.mult, op1=ALU.add)
                    if i < len(heads) - 1:
                        chain(ins)
                ins.then_inc(S.relu_used, 1)
                dve.wait_ge(S.relu_used, u + 1)
            chain(nc.vector.tensor_tensor(score, score, C(C_M2, 3 * P), ALU.add))
            for r in range(TOPK // 8):
                views = ((score[:, 0:P], m8[:, 0:8]), (score[:, P:3 * P], m8[:, 8:16]))
                for v, m in views:
                    ins = nc.vector.max(m, v)
                    ins.then_inc(S.dve_chain, 1)
                    chain.n += 1
                dve.wait_ge(S.dve_chain, chain.n)
                for v, m in views:
                    ins = nc.vector.match_replace(v, m, v, PICKED)
                    ins.then_inc(S.dve_chain, 1)
                    chain.n += 1
                dve.wait_ge(S.dve_chain, chain.n)
            chain(nc.vector.tensor_scalar(dsa_mask, score, PICKED / 2, NEG, ALU.is_gt, ALU.mult))
            chain(nc.vector.tensor_tensor(dsa_mask, dsa_mask, C(C_M2, 3 * P), ALU.add))

            def soften(n):
                p, at = prob[n % 2], 4 * (n % 2)
                mask = C(C_M2, 3 * P) if n < HA else dsa_mask
                dve.wait_ge(S.scores_done, n + 1)
                if n >= 2:
                    dve.wait_ge(S.pt_done, n - 1)
                nc.vector.scalar_tensor_tensor(out=p[:, 0:3 * P], in0=ps[:, 4 + n % 2, 0:3 * P], scalar=HD ** -0.5,
                                               in1=mask, op0=ALU.mult, op1=ALU.add).then_inc(S.scores_read, 1)
                dve.wait_ge(S.scores_read, n + 1)
                nc.vector.tensor_reduce(small[:, at:at + 1], p[:, 0:P], AX.X, ALU.max, negate=True)
                nc.vector.tensor_reduce(small[:, at + 1:at + 2], p[:, P:3 * P], AX.X, ALU.max,
                                        negate=True).then_inc(S.max_ready, 1)

            def normalise(n):
                p, at = prob[n % 2], 4 * (n % 2)
                dve.wait_ge(S.exp_ready, n + 1)
                chain(nc.vector.reciprocal(small[:, at + 2:at + 4], small[:, at + 2:at + 4]))
                nc.vector.tensor_scalar(p[:, 0:P], p[:, 0:P], small[:, at + 2:at + 3], None, ALU.mult)
                nc.vector.tensor_scalar(p[:, P:3 * P], p[:, P:3 * P], small[:, at + 3:at + 4], None,
                                        ALU.mult).then_inc(S.probs_ready, 1)

            for n in range(HEADS_2 + 1):
                if n < HEADS_2:
                    soften(n)
                    dve.wait_ge(S.z_done, n + 1)
                    nc.vector.scalar_tensor_tensor(out=st[:, n % 2, :], in0=ps[:, n % 2, 0:3 * P], scalar=HD ** -0.5,
                                                   in1=C(C_M3, 3 * P), op0=ALU.mult,
                                                   op1=ALU.add).then_inc(S.zm_ready, 1)
                    normalise(n)
                    dve.wait_ge(S.soft_ready, n + 1)
                    if n >= 2:
                        dve.wait_ge(S.cum_done, n - 1)
                    nc.vector.scalar_tensor_tensor(out=st[:, 4 + n % 2, :], in0=st[:, n % 2, :], scalar=0.0,
                                                   in1=st[:, 2 + n % 2, :], op0=ALU.max,
                                                   op1=ALU.add).then_inc(S.l_ready, 1)
                if n >= 1:
                    i = n - 1
                    dve.wait_ge(S.cum_done, i + 1)
                    if i >= 2:
                        dve.wait_ge(S.o_done, i - 1)
                    nc.vector.tensor_tensor(st[:, 6 + i % 2, :], st[:, i % 2, :], ps[:, 2, 0:3 * P],
                                            ALU.subtract).then_inc(S.arg_ready, 1)
            vv, rr = (e[:].rearrange("p k t -> p (k t)") for e in e_buf)
            dve.wait_ge(S.o_ss, 1)
            nc.vector.tensor_scalar(vv, ps[:, 4:8, :].rearrange("p b t -> p (b t)"), 1.0 / HD, EPS,
                                    ALU.mult, ALU.add).then_inc(S.o_var, 1)
            dve.wait_ge(S.o_rstd, 1)
            refine(chain, rr, vv)
            for k in range(KD):
                ins = nc.vector.scalar_tensor_tensor(out=hk[:, k, :], in0=hk[:, k, :],
                                                     scalar=v_now[:, V2_OUT + k:V2_OUT + k + 1],
                                                     in1=e_buf[1][:, k, :], op0=ALU.mult, op1=ALU.mult)
            ins.then_inc(S.o_ready, 1)
            dve.wait_ge(S.tile_done, Z_LATE + N_LATE)
            add_bias(5, 9, ps[:, 2, LATE_AT:LATE_AT + 2 * N_LATE])
            dve.sem_inc(S.mod_ready, 1)
            gain(2)
            chain(nc.vector.tensor_scalar(parts[8], parts[8], 0.5, None, ALU.mult))
            first_low(dve, FFN_D, 1, (0,))
            residual(dve, lambda b: Z_O + b, 0, parts[5])
            norm_dve(dve, chain, 2, 8, parts[7], parts[6], split=True)
            ffn_dve(dve, FFN_D, 1, 1)
            residual(dve, lambda b: FFN_D + FFN_TILES - 1, 4, parts[8])

        def two_pool(pool, l):
            for j, (at, n) in enumerate(ropes):
                r = HD if n == 1 else P
                part = fq[0:r, at:at + n, :]
                if j >= NORMED:
                    pool.wait_ge(S.head_ready, j - NORMED + 1)
                else:
                    pool.wait_ge(S.evac_done, j + 1)
                if j >= 1:
                    pool.wait_ge(S.rope_done, j)
                nc.gpsimd.tensor_tensor(rope_a[0:r, 0:n, :], part,
                                        con_sb[0:r, C_COS:C_COS + T].unsqueeze(1).broadcast_to([r, n, T]),
                                        ALU.mult).then_inc(S.pool_chain, 1)
                pool.wait_ge(S.pool_chain, j + 1)
                pool.wait_ge(S.rot_scaled, j + 1)
                nc.gpsimd.tensor_tensor(part, rope_a[0:r, 0:n, :], rope_b[0:r, 0:n, :],
                                        ALU.add).then_inc(S.rope_done, 1)

        with nc.Fori(0, DEPTH) as l:
            with nc.Block() as block:
                @block.sync
                def _(sp):
                    stream_in(sp, l, TILES_2, DEPTH * TILES_1, True)

                @block.tensor
                def _(pe):
                    two_pe(pe, l)

                @block.scalar
                def _(act):
                    two_act(act, l)

                @block.vector
                def _(dve):
                    two_dve(dve, l)

                @block.gpsimd
                def _(pool):
                    two_pool(pool, l)
            nc.all_engine_barrier(sems_to_clear=layer_sems)


        with nc.Block() as block:
            @block.sync
            def _(sp):
                sp.dma_start(out.rearrange("(k p) t -> p k t", p=P), x[:]).then_inc(S.store, 16)
                sp.wait_ge(S.store, 16)




def constants():
    c = np.zeros((P, C_W + C_NEXT), np.float32)
    i = np.arange(P)
    c[i, C_ID + i] = 1
    c[:, C_ONE:C_ONE + P] = 1
    c[:, C_BD:C_BD + P] = (i[:, None] // HD == i[None, :] // HD)
    half = DH // 2
    c[i[:half] + half, C_R1 + i[:half]] = -1
    c[i[:half], C_R1 + half + i[:half]] = 1
    r = ROPE_DIM // 2
    for base in (0, HD):
        for d in range(r):
            c[base + d + r, C_R2 + base + d] = -1
            c[base + d, C_R2 + base + d + r] = 1
    c[:, C_TRI:C_TRI + P] = (i[:, None] >= i[None, :])
    t = np.arange(T)
    for g, (window, dil) in enumerate(GROUPS):
        back = t[:, None] - t[None, :]
        ok = (back >= 0) & (back <= window) & (back % dil == 0)
        m = np.where(ok, 0.0, NEG)
        c[:, C_M1 + g * P:C_M1 + (g + 1) * P] = m[:P, :P]
        c[:, C_M1 + NG * P + g * T:C_M1 + NG * P + (g + 1) * T] = m[P:, :]
    n_m2, n_m3, n_cos, n_sin = (at + C_NEXT for at in (C_M2, C_M3, C_COS, C_SIN))
    m = np.where(t[:, None] >= t[None, :], 0.0, NEG)
    c[:, n_m2:n_m2 + P] = m[:P, :P]
    c[:, n_m2 + P:n_m2 + 3 * P] = m[P:, :]
    m = np.where(t[:, None] < t[None, :], 0.0, NEG)
    c[:, n_m3:n_m3 + T] = m[:P, :]
    c[:, n_m3 + T:n_m3 + 3 * P] = m[P:, P:]
    inv = np.float32(500000.0) ** (-np.arange(0, ROPE_DIM, 2, dtype=np.float32) / np.float32(ROPE_DIM))
    ang = t.astype(np.float32)[None, :] * inv[:, None].astype(np.float32)
    c[:, n_cos:n_cos + T] = 1
    for base in (0, r, HD, HD + r):
        c[base:base + r, n_cos:n_cos + T] = np.cos(ang)
        c[base:base + r, n_sin:n_sin + T] = np.sin(ang)
    lm = np.zeros((P, LEVELS, P), np.float32)
    for n in range(1, LEVELS):
        hf = P >> n
        same = i[:, None] // (2 * hf) == i[None, :] // (2 * hf)
        lm[:, n - 1, :] = same & (i[:, None] % (2 * hf) < hf) & (i[None, :] % (2 * hf) >= hf)
    lm[:, LEVELS - 1, :] = i[:, None] == i[None, :]
    return c, lm.reshape(P, LEVELS * P)


def columns(v):
    v = np.asarray(v)
    return np.moveaxis(v.reshape(*v.shape[:-1], -1, P), -1, 0)


def by_columns(w):
    n = w.shape[1] // T
    return w.reshape(KD, P, n, T).transpose(2, 1, 0, 3).reshape(n, P, TILE)


def by_ffn(gate, up, down):
    g, u = by_columns(gate), by_columns(up)
    d = down.reshape(CHUNKS, 2, P, D).transpose(0, 2, 1, 3).reshape(CHUNKS, P, TILE)
    tiles = [g[0], u[0]]
    for i in range(1, CHUNKS):
        tiles += [g[i], u[i], d[i - 1]]
    return tiles + [d[CHUNKS - 1]]


def layer_one(a, l):
    w = a["w_in"][l]
    aw = NG * HEADS * DH
    q, k, v = w[:, :aw], w[:, aw:2 * aw], w[:, 2 * aw:3 * aw]
    qb, fb, ib, og, ga, gb = (w[:, 3 * aw + i * D:3 * aw + (i + 1) * D] for i in range(6))
    gu = a["ffn1_w_gu"][l]
    tiles = by_ffn(gu[:, :D_FF], gu[:, D_FF:], a["ffn1_w_down"][l])
    for part in (fb, qb, ib, q, k, v, og, ga, gb, a["w_hgrn_branch"][l]):
        tiles += list(by_columns(part))
    tiles += list(a["w_att_branch"][l].reshape(HEADS, P, 2, 512).transpose(2, 1, 0, 3).reshape(2, P, TILE))
    kv = list(by_columns(a["xattn_wkv"][l]))
    tiles += kv[:2] + list(by_columns(a["w_mix_out"][l])) + kv[2:]
    tiles += list(by_columns(a["xattn_wq"][l])) + list(by_columns(a["xattn_wo"][l]))
    gu = a["ffn2_w_gu"][l]
    tiles += by_ffn(gu[:, :D_FF], gu[:, D_FF:], a["ffn2_w_down"][l])
    assert len(tiles) == TILES_1
    return tiles


def layer_two(a, l):
    w = a["w_in_2"][l]
    names = ("qa", "ka", "va", "qb", "kb", "vb", "qi", "ki", "wi", "qc", "kc", "vc")
    sizes = (HA * HD,) * 3 + (HB * HD,) * 3 + (IDX * HD, HD, IDX) + (HC * HD,) * 3
    part, at = {}, 0
    for name, size in zip(names, sizes):
        part[name] = w[:, at:at + size]
        at += size
    ki = np.zeros((D, T), w.dtype)
    ki[:, :HD], ki[:, HD:HD + IDX] = part["ki"], part["wi"]
    ada = list(by_columns(a["w_ada_2"][l]))
    tiles = ada[:N_FRONT]
    tiles += by_ffn(a["ffn_w1_2"][l, 0], a["ffn_w3_2"][l, 0], a["ffn_w2_2"][l, 0])
    tiles += ada[N_FRONT:N_FRONT + N_MID]
    for w_ in (part["qi"], ki, part["qb"], part["kb"], part["qa"], part["ka"], part["va"], part["vb"],
               part["vc"], part["qc"], part["kc"]):
        tiles += list(by_columns(w_))
    tiles += ada[N_FRONT + N_MID:] + list(by_columns(a["w_out_2"][l]))
    tiles += by_ffn(a["ffn_w1_2"][l, 1], a["ffn_w3_2"][l, 1], a["ffn_w2_2"][l, 1])
    assert len(tiles) == TILES_2
    return tiles


def vectors(a):
    cols = []
    for l in range(DEPTH):
        cols += [columns(a[n][l]) for n in ("ffn1_norm", "mix_norm", "hgrn_head_norm", "xattn_norm", "mem_norm",
                                            "ffn2_norm")]
    for l in range(DEPTH):
        cols += [columns(a["norm_g_2"][l]).reshape(P, 3 * KD), columns(a["out_g_2"][l])]
        cols += [np.concatenate([a["qk_g_2"][l].T] * 2, axis=0)]
        cols += [columns(a["b_ada_2"][l])]
    cols += [columns(a["hgrn_lower_bounds"]).reshape(P, DEPTH * KD), columns(a["final_norm"])]
    cols += [columns(a["c_2"][0])]
    inv = np.float32(10000.0) ** (-np.arange(0, DH, 2, dtype=np.float32) / np.float32(DH))
    cols += [np.concatenate([inv, inv]).astype(np.float32)[:, None]]
    out = np.concatenate(cols, axis=1)
    assert out.shape[1] == VEC_W
    return np.ascontiguousarray(out)


def kernel(**inputs):
    import concourse.bacc as bacc
    from concourse.bass_utils import run_bass_kernel_spmd as run

    a = {k: np.asarray(v) for k, v in inputs.items()}
    tiles = []
    for l in range(DEPTH):
        tiles += layer_one(a, l)
    for l in range(DEPTH):
        tiles += layer_two(a, l)
    con, lm = constants()
    arrays = {
        "x_t": np.ascontiguousarray(a["x"][0].T), "mem_t": np.ascontiguousarray(a["mem"][0].T),
        "pos": np.ascontiguousarray(a["positions"]), "stream": np.stack(tiles), "vec": vectors(a),
        "con": con, "lmask": lm,
    }
    nc = bacc.Bacc("TRN2", target_bir_lowering=False, num_devices=1)
    args = [nc.dram_tensor(n, v.shape, mybir.dt.from_np(v.dtype), kind="ExternalInput").ap()
            for n, v in arrays.items()]
    args.append(nc.dram_tensor("out_t", (D, T), F32, kind="ExternalOutput").ap())
    program(nc, *args)
    r = run(nc, [arrays], core_ids=[0])
    return np.ascontiguousarray(r.results[0]["out_t"].T)[None]
```
